# Optimizing a Trainium2 kernel written in Bass

```python
import math
import jax, jax.numpy as jnp
from jax import lax
import numpy as np
import jax
import jax.numpy as jnp

D_MODEL = 1024
BATCH = 1
SEQ = 1024
DEPTH = 2

N_EVEN = (DEPTH + 1) // 2
N_ODD = DEPTH // 2
EPS = 1e-6

CONF_WIDTH = D_MODEL // 2
CONF_KERNEL = 31
LRU_WIDTH = D_MODEL // 2
LRU_HEADS = 8
LRU_HEAD_DIM = LRU_WIDTH // LRU_HEADS
LRU_CONV = 4
LRU_C = 8.0
AB_IN = 2 * CONF_WIDTH + 2 * LRU_WIDTH
AB_OUT = CONF_WIDTH + LRU_WIDTH
ML_HEADS = 8
ML_V_DIM = D_MODEL
ML_HEAD_V = ML_V_DIM // ML_HEADS
ML_HEAD_QK = ML_HEAD_V // 2
ML_QK_DIM = ML_HEADS * ML_HEAD_QK
ML_CHUNK = 64
ML_IN = 2 * ML_QK_DIM + 2 * ML_V_DIM + 2 * ML_HEADS
D_FF = int(math.ceil(8 * D_MODEL / 3 / 256)) * 256


def _rmsnorm(x, g):
    xf = x.astype(jnp.float32)
    y = xf * lax.rsqrt(jnp.mean(xf * xf, axis=-1, keepdims=True) + EPS)
    return (y * g.astype(jnp.float32)).astype(x.dtype)

def _layernorm(x, g, b):
    xf = x.astype(jnp.float32)
    mu = jnp.mean(xf, axis=-1, keepdims=True)
    var = jnp.mean(jnp.square(xf - mu), axis=-1, keepdims=True)
    y = (xf - mu) * lax.rsqrt(var + EPS)
    return (y * g.astype(jnp.float32) + b.astype(jnp.float32)).astype(x.dtype)

def _causal_dwconv(x, w, b):
    k = w.shape[0]
    c = x.shape[-1]
    y = lax.conv_general_dilated(
        x, w[:, None, :].astype(x.dtype), window_strides=(1,), padding=[(k - 1, 0)],
        dimension_numbers=('NWC', 'WIO', 'NWC'), feature_group_count=c)
    return y + b

def _conformer_conv(u, conv_w, conv_b, ln_g, ln_b):
    val, gate = jnp.split(u, 2, axis=-1)
    y = val * jax.nn.sigmoid(gate)
    y = _causal_dwconv(y, conv_w, conv_b)
    return jax.nn.silu(_layernorm(y, ln_g, ln_b))

def _lru_combine(left, right):
    a_l, b_l = left
    a_r, b_r = right
    return a_l * a_r, a_r * b_l + b_r

def _rglru_block(u, conv_w, conv_b, w_a, b_a, w_x, b_x, lam):
    bsz, seq, _ = u.shape
    gate_in, rec_in = jnp.split(u, 2, axis=-1)
    xr = _causal_dwconv(rec_in, conv_w, conv_b)
    xh = xr.reshape(bsz, seq, LRU_HEADS, LRU_HEAD_DIM)
    r = jax.nn.sigmoid(jnp.einsum('bshd,hde->bshe', xh, w_a) + b_a)
    i = jax.nn.sigmoid(jnp.einsum('bshd,hde->bshe', xh, w_x) + b_x)
    log_base = -jax.nn.softplus(-lam.astype(jnp.float32)).reshape(LRU_HEADS, LRU_HEAD_DIM)
    log_a = LRU_C * log_base * r.astype(jnp.float32)
    a = jnp.exp(log_a)
    gated_x = jnp.sqrt(-jnp.expm1(2.0 * log_a)) * (i * xh).astype(jnp.float32)
    _, h = lax.associative_scan(_lru_combine, (a, gated_x), axis=1)
    h = h.reshape(bsz, seq, LRU_WIDTH).astype(u.dtype)
    return h * jax.nn.gelu(gate_in)

def _ab_mixer(xn, w_in, b_in, conf_conv_w, conf_conv_b, conf_ln_g, conf_ln_b,
              lru_conv_w, lru_conv_b, lru_w_a, lru_b_a, lru_w_x, lru_b_x, lru_lambda, w_out):
    u = jnp.einsum('bsd,de->bse', xn, w_in) + b_in
    u_conf, u_lru = jnp.split(u, [2 * CONF_WIDTH], axis=-1)
    y_a = _conformer_conv(u_conf, conf_conv_w, conf_conv_b, conf_ln_g, conf_ln_b)
    y_b = _rglru_block(u_lru, lru_conv_w, lru_conv_b, lru_w_a, lru_b_a, lru_w_x, lru_b_x, lru_lambda)
    y = jnp.concatenate([y_a, y_b], axis=-1)
    return jnp.einsum('bse,ed->bsd', y, w_out)

def _mlstm_chunk_step(carry, inp):
    c_state, n_state, m_state = carry
    qc, kc, vc, ic, lfc = inp
    L = qc.shape[2]
    causal = jnp.tril(jnp.ones((L, L), dtype=bool))
    b = jnp.cumsum(lfc, axis=-1)
    log_d = b[..., :, None] - b[..., None, :] + ic[..., None, :]
    log_d = jnp.where(causal, log_d, -jnp.inf)
    log_inter = b + m_state[..., None]
    m_row = jnp.maximum(log_inter, jnp.max(log_d, axis=-1))
    d_w = jnp.exp(log_d - m_row[..., None])
    inter_w = jnp.exp(log_inter - m_row)
    scores = jnp.einsum('bhjd,bhsd->bhjs', qc, kc) * d_w
    num = jnp.einsum('bhjs,bhsv->bhjv', scores, vc) + inter_w[..., None] * jnp.einsum('bhjd,bhdv->bhjv', qc, c_state)
    den = jnp.sum(scores, axis=-1) + inter_w * jnp.einsum('bhjd,bhd->bhj', qc, n_state)
    h = num / jnp.maximum(jnp.abs(den), jnp.exp(-m_row))[..., None]
    b_last = b[..., -1]
    log_w = b_last[..., None] - b + ic
    m_new = jnp.maximum(b_last + m_state, jnp.max(log_w, axis=-1))
    w_s = jnp.exp(log_w - m_new[..., None])
    decay = jnp.exp(b_last + m_state - m_new)
    c_new = decay[..., None, None] * c_state + jnp.einsum('bhsd,bhsv->bhdv', w_s[..., None] * kc, vc)
    n_new = decay[..., None] * n_state + jnp.einsum('bhs,bhsd->bhd', w_s, kc)
    return (c_new, n_new, m_new), h

def _mlstm_mixer(xn, w_in, b_in, head_g, w_out):
    bsz, seq, _ = xn.shape
    nc = seq // ML_CHUNK
    u = jnp.einsum('bsd,de->bse', xn, w_in) + b_in
    q, k, v, o, ig, fg = jnp.split(
        u, [ML_QK_DIM, 2 * ML_QK_DIM, 2 * ML_QK_DIM + ML_V_DIM,
            2 * ML_QK_DIM + 2 * ML_V_DIM, 2 * ML_QK_DIM + 2 * ML_V_DIM + ML_HEADS], axis=-1)
    f32 = jnp.float32

    def to_chunks(t, d):
        return t.astype(f32).reshape(bsz, nc, ML_CHUNK, ML_HEADS, d).transpose(1, 0, 3, 2, 4)

    def gate_chunks(t):
        return t.astype(f32).reshape(bsz, nc, ML_CHUNK, ML_HEADS).transpose(1, 0, 3, 2)

    qc = to_chunks(q, ML_HEAD_QK)
    kc = to_chunks(k, ML_HEAD_QK) * (ML_HEAD_QK ** -0.5)
    vc = to_chunks(v, ML_HEAD_V)
    ic = gate_chunks(ig)
    lfc = gate_chunks(jax.nn.log_sigmoid(fg))
    init = (jnp.zeros((bsz, ML_HEADS, ML_HEAD_QK, ML_HEAD_V), f32),
            jnp.zeros((bsz, ML_HEADS, ML_HEAD_QK), f32),
            jnp.zeros((bsz, ML_HEADS), f32))
    _, h = lax.scan(_mlstm_chunk_step, init, (qc, kc, vc, ic, lfc))
    h = h.transpose(1, 0, 3, 2, 4).reshape(bsz, seq, ML_HEADS, ML_HEAD_V)
    h = h * lax.rsqrt(jnp.mean(h * h, axis=-1, keepdims=True) + EPS)
    h = (h.reshape(bsz, seq, ML_V_DIM) * head_g.astype(f32)).astype(xn.dtype)
    h = jax.nn.sigmoid(o) * h
    return jnp.einsum('bse,ed->bsd', h, w_out)

def _swiglu(xn, w_gate, w_up, w_down):
    g = jnp.einsum('bsd,df->bsf', xn, w_gate)
    up = jnp.einsum('bsd,df->bsf', xn, w_up)
    return jnp.einsum('bsf,fd->bsd', jax.nn.silu(g) * up, w_down)

def first_inputs(seed: int = 0) -> dict:
    key = jax.random.key(seed)
    ks = iter(jax.random.split(key, 40))

    def nrm(shape, scale):
        return jax.random.normal(next(ks), shape, jnp.float32) * scale

    def gain(shape):
        return 1.0 + nrm(shape, 0.05)

    lam_u = jax.random.uniform(next(ks), (N_EVEN, LRU_WIDTH), jnp.float32, minval=0.9, maxval=0.999)
    lam_base = lam_u ** (1.0 / LRU_C)
    lru_lambda = jnp.log(lam_base) - jnp.log1p(-lam_base)

    ml_b_in = nrm((N_ODD, ML_IN), 0.02)
    f_bias = jnp.linspace(3.0, 6.0, ML_HEADS, dtype=jnp.float32) + nrm((N_ODD, ML_HEADS), 0.1)
    ml_b_in = ml_b_in.at[:, ML_IN - ML_HEADS:].set(f_bias)

    return {
        'x': nrm((BATCH, SEQ, D_MODEL), 1.0),
        'pre_mix_g': gain((DEPTH, D_MODEL)),
        'post_mix_g': gain((DEPTH, D_MODEL)),
        'pre_ffn_g': gain((DEPTH, D_MODEL)),
        'post_ffn_g': gain((DEPTH, D_MODEL)),
        'ab_w_in': nrm((N_EVEN, D_MODEL, AB_IN), D_MODEL ** -0.5),
        'ab_b_in': nrm((N_EVEN, AB_IN), 0.02),
        'conf_conv_w': nrm((N_EVEN, CONF_KERNEL, CONF_WIDTH), CONF_KERNEL ** -0.5),
        'conf_conv_b': nrm((N_EVEN, CONF_WIDTH), 0.02),
        'conf_ln_g': gain((N_EVEN, CONF_WIDTH)),
        'conf_ln_b': nrm((N_EVEN, CONF_WIDTH), 0.02),
        'lru_conv_w': nrm((N_EVEN, LRU_CONV, LRU_WIDTH), LRU_CONV ** -0.5),
        'lru_conv_b': nrm((N_EVEN, LRU_WIDTH), 0.02),
        'lru_w_a': nrm((N_EVEN, LRU_HEADS, LRU_HEAD_DIM, LRU_HEAD_DIM), LRU_HEAD_DIM ** -0.5),
        'lru_b_a': nrm((N_EVEN, LRU_HEADS, LRU_HEAD_DIM), 0.02),
        'lru_w_x': nrm((N_EVEN, LRU_HEADS, LRU_HEAD_DIM, LRU_HEAD_DIM), LRU_HEAD_DIM ** -0.5),
        'lru_b_x': nrm((N_EVEN, LRU_HEADS, LRU_HEAD_DIM), 0.02),
        'lru_lambda': lru_lambda,
        'ab_w_out': nrm((N_EVEN, AB_OUT, D_MODEL), AB_OUT ** -0.5),
        'ml_w_in': nrm((N_ODD, D_MODEL, ML_IN), D_MODEL ** -0.5),
        'ml_b_in': ml_b_in,
        'ml_head_g': gain((N_ODD, ML_V_DIM)),
        'ml_w_out': nrm((N_ODD, ML_V_DIM, D_MODEL), ML_V_DIM ** -0.5),
        'ffn_w_gate': nrm((DEPTH, D_MODEL, D_FF), D_MODEL ** -0.5),
        'ffn_w_up': nrm((DEPTH, D_MODEL, D_FF), D_MODEL ** -0.5),
        'ffn_w_down': nrm((DEPTH, D_FF, D_MODEL), D_FF ** -0.5),
    }

def first_block(x, pre_mix_g, post_mix_g, pre_ffn_g, post_ffn_g,
              ab_w_in, ab_b_in, conf_conv_w, conf_conv_b, conf_ln_g, conf_ln_b,
              lru_conv_w, lru_conv_b, lru_w_a, lru_b_a, lru_w_x, lru_b_x, lru_lambda, ab_w_out,
              ml_w_in, ml_b_in, ml_head_g, ml_w_out,
              ffn_w_gate, ffn_w_up, ffn_w_down):
    for layer in range(DEPTH):
        j = layer // 2
        h = _rmsnorm(x, pre_mix_g[layer])
        if layer % 2 == 0:
            h = _ab_mixer(h, ab_w_in[j], ab_b_in[j], conf_conv_w[j], conf_conv_b[j],
                          conf_ln_g[j], conf_ln_b[j], lru_conv_w[j], lru_conv_b[j],
                          lru_w_a[j], lru_b_a[j], lru_w_x[j], lru_b_x[j], lru_lambda[j], ab_w_out[j])
        else:
            h = _mlstm_mixer(h, ml_w_in[j], ml_b_in[j], ml_head_g[j], ml_w_out[j])
        x = x + _rmsnorm(h, post_mix_g[layer])
        h = _swiglu(_rmsnorm(x, pre_ffn_g[layer]), ffn_w_gate[layer], ffn_w_up[layer], ffn_w_down[layer])
        x = x + _rmsnorm(h, post_ffn_g[layer])
    return x


DEPTH_2 = 1

N_MIXERS = 4
MIX_WIDTH = 256
HEAD_DIM = 64
N_HEADS = 4
NORM_EPS = 1e-6
NEG_INF = -1e30

GDN_CONV = 4
GDN_CHUNK = 64

SG_CHUNK = 128
SG_GROUPS = 4
SG_GROUP_DIM = MIX_WIDTH // SG_GROUPS

RWKV_DECAY_RANK = 64
RWKV_A_RANK = 64
RWKV_GN_EPS = 64e-5
RW_WIDTH = 3 * MIX_WIDTH + RWKV_DECAY_RANK + RWKV_A_RANK

NSA_KV_DIM = HEAD_DIM
NSA_CMP_LEN = 32
NSA_CMP_STRIDE = 16
NSA_CMP_RATIO = NSA_CMP_LEN // NSA_CMP_STRIDE
NSA_CMP_HIDDEN = 64
NSA_SEL_BLOCK = 64
NSA_N_SEL = 8
NSA_FORCE_BONUS = 1e4
NSA_WINDOW = 256
NSA_Q_BLOCK = 128
NSA_SEL_Q_BLOCK = 64

IN_SPLITS = (
    3 * MIX_WIDTH,
    N_HEADS,
    N_HEADS,
    MIX_WIDTH,
    MIX_WIDTH,
    MIX_WIDTH,
    MIX_WIDTH,
    RW_WIDTH,
    MIX_WIDTH,
    MIX_WIDTH,
    6 * NSA_KV_DIM,
    3 * N_HEADS,
    MIX_WIDTH,
    N_MIXERS * D_MODEL,
)
IN_OFFSETS = tuple(sum(IN_SPLITS[: i + 1]) for i in range(len(IN_SPLITS) - 1))
D_IN = sum(IN_SPLITS)
ALIBI_SLOPES = tuple(2.0 ** (-8.0 * (h + 1) / N_HEADS) for h in range(N_HEADS))


def rmsnorm(x, gain, eps=NORM_EPS):
    x32 = x.astype(jnp.float32)
    y = x32 * lax.rsqrt(jnp.mean(x32 * x32, axis=-1, keepdims=True) + eps)
    return (y * gain.astype(jnp.float32)).astype(x.dtype)

def layernorm(x, gain, bias, eps):
    x32 = x.astype(jnp.float32)
    xc = x32 - jnp.mean(x32, axis=-1, keepdims=True)
    y = xc * lax.rsqrt(jnp.mean(xc * xc, axis=-1, keepdims=True) + eps)
    return (y * gain.astype(jnp.float32) + bias.astype(jnp.float32)).astype(x.dtype)

def l2norm(x, eps=1e-6):
    x32 = x.astype(jnp.float32)
    return (x32 * lax.rsqrt(jnp.sum(x32 * x32, axis=-1, keepdims=True) + eps)).astype(x.dtype)

def shift_prev(x):
    return jnp.pad(x, ((0, 0), (1, 0), (0, 0)))[:, :-1]

def causal_depthwise_conv(x, w):
    width, ch = w.shape
    return lax.conv_general_dilated(
        x, w[:, None, :].astype(x.dtype), window_strides=(1,),
        padding=((width - 1, 0),), dimension_numbers=('NWC', 'WIO', 'NWC'),
        feature_group_count=ch)

def masked_softmax(s, mask):
    p = jax.nn.softmax(jnp.where(mask, s, NEG_INF), axis=-1)
    return jnp.where(mask, p, 0.0)

def chunked_gated_delta_rule(q, k, v, g, beta):
    B, T, H, E = q.shape
    C = GDN_CHUNK
    N = T // C

    def chunks(t):
        t = t.reshape((B, N, C, H) + t.shape[3:])
        return jnp.moveaxis(t, (1, 3), (0, 2))

    q, k, v, g, beta = (chunks(t) for t in (q, k, v, g, beta))
    gc = jnp.cumsum(g, axis=-1)
    pos = jnp.arange(C)
    causal = pos[:, None] >= pos[None, :]
    strict = pos[:, None] > pos[None, :]
    decay = jnp.where(causal, jnp.exp(jnp.where(causal, gc[..., :, None] - gc[..., None, :], 0.0)), 0.0)
    kb = k * beta[..., None]
    a_mat = jnp.where(strict, jnp.einsum('nbhcd,nbhed->nbhce', kb, k) * decay, 0.0)
    eye = jnp.eye(C, dtype=q.dtype)
    t_inv = lax.linalg.triangular_solve(eye + a_mat, jnp.broadcast_to(eye, a_mat.shape),
                                        left_side=True, lower=True, unit_diagonal=True)
    u = t_inv @ (v * beta[..., None])
    w = t_inv @ (kb * jnp.exp(gc)[..., None])
    attn = jnp.einsum('nbhcd,nbhed->nbhce', q, k) * decay
    g_last = gc[..., -1]
    q_in = q * jnp.exp(gc)[..., None]
    k_out = k * jnp.exp(g_last[..., None] - gc)[..., None]

    def step(state, xs):
        u_n, w_n, attn_n, q_n, k_n, gl_n = xs
        v_new = u_n - w_n @ state
        o_n = q_n @ state + attn_n @ v_new
        state = state * jnp.exp(gl_n)[..., None, None] + jnp.swapaxes(k_n, -1, -2) @ v_new
        return state, o_n

    state0 = jnp.zeros((B, H, E, v.shape[-1]), q.dtype)
    _, o = lax.scan(step, state0, (u, w, attn, q_in, k_out, g_last))
    return jnp.moveaxis(o, (0, 2), (1, 3)).reshape(B, T, H, -1)

def gated_deltanet(qkv, a_logit, b_logit, z, conv_w, a_log, dt_bias, norm_w):
    B, T, _ = qkv.shape
    f32 = jnp.float32
    qkv = jax.nn.silu(causal_depthwise_conv(qkv, conv_w))
    q, k, v = jnp.split(qkv, 3, axis=-1)
    heads = lambda t: t.reshape(B, T, N_HEADS, HEAD_DIM).astype(f32)
    q = l2norm(heads(q)) * (HEAD_DIM ** -0.5)
    k = l2norm(heads(k))
    v = heads(v)
    beta = jax.nn.sigmoid(b_logit.astype(f32))
    g = -jnp.exp(a_log.astype(f32)) * jax.nn.softplus(a_logit.astype(f32) + dt_bias.astype(f32))
    o = chunked_gated_delta_rule(q, k, v, g, beta)
    o = rmsnorm(o, norm_w) * jax.nn.silu(heads(z))
    return o.reshape(B, T, MIX_WIDTH).astype(qkv.dtype)

def spatial_gating(u, v, z, ln_gain, ln_bias, w_s, b_s):
    B, T, _ = u.shape
    u = jax.nn.gelu(u)
    v = jax.nn.gelu(v).reshape(B, T, SG_GROUPS, SG_GROUP_DIM)
    v = layernorm(v, ln_gain.reshape(SG_GROUPS, SG_GROUP_DIM), ln_bias.reshape(SG_GROUPS, SG_GROUP_DIM), 1e-5)
    v = v.reshape(B, T // SG_CHUNK, SG_CHUNK, SG_GROUPS, SG_GROUP_DIM)
    tril = jnp.tril(jnp.ones((SG_CHUNK, SG_CHUNK), dtype=bool))
    w_c = jnp.where(tril, w_s, 0.0).astype(v.dtype)
    mixed = jnp.einsum('gts,bnsgc->bntgc', w_c, v) + b_s.T[:, :, None].astype(v.dtype)
    s = u * mixed.reshape(B, T, MIX_WIDTH)
    return s * jax.nn.silu(z)

def rwkv7_scan(r, w, k, v, kk, a):
    def step(S, xs):
        r_t, w_t, k_t, v_t, kk_t, a_t = xs
        sa = jnp.einsum('bhvk,bhk->bhv', S, -kk_t)
        S = (S * w_t[:, :, None, :] + sa[..., None] * (kk_t * a_t)[:, :, None, :]
             + v_t[..., None] * k_t[:, :, None, :])
        return S, jnp.einsum('bhvk,bhk->bhv', S, r_t)

    B, T, H, E = r.shape
    xs = tuple(jnp.moveaxis(t, 1, 0) for t in (r, w, k, v, kk, a))
    _, o = lax.scan(step, jnp.zeros((B, H, E, E), jnp.float32), xs)
    return jnp.moveaxis(o, 0, 1)

def rwkv7_time_mix(rw, z, mu, w_up, w0, a_up, a0, k_k, k_a, r_k, gn_gain, gn_bias):
    B, T, _ = rw.shape
    f32 = jnp.float32
    rw = (rw + mu * (shift_prev(rw) - rw)).astype(f32)
    r, k, v, wd, ad = jnp.split(
        rw, (MIX_WIDTH, 2 * MIX_WIDTH, 3 * MIX_WIDTH, 3 * MIX_WIDTH + RWKV_DECAY_RANK), axis=-1)
    w_log = -jax.nn.softplus(-(w0.astype(f32) + jnp.tanh(wd) @ w_up.astype(f32))) - 0.5
    decay = jnp.exp(-jnp.exp(w_log))
    a = jax.nn.sigmoid(a0.astype(f32) + ad @ a_up.astype(f32))
    heads = lambda t: t.reshape(B, T, N_HEADS, HEAD_DIM)
    kk = l2norm(heads(k * k_k.astype(f32)))
    k = k * (1.0 + (a - 1.0) * k_a.astype(f32))
    r_h, k_h, v_h = heads(r), heads(k), heads(v)
    o = rwkv7_scan(r_h, heads(decay), k_h, v_h, kk, heads(a))
    o = layernorm(o, gn_gain.reshape(N_HEADS, HEAD_DIM), gn_bias.reshape(N_HEADS, HEAD_DIM), RWKV_GN_EPS)
    o = o + jnp.sum(r_h * k_h * r_k.astype(f32), axis=-1, keepdims=True) * v_h
    return (o.reshape(B, T, MIX_WIDTH) * jax.nn.silu(z.astype(f32))).astype(z.dtype)

def compress_blocks(x, pos_emb, w1, w2):
    B, T, E = x.shape
    ns = T // NSA_CMP_STRIDE
    nc = ns - NSA_CMP_RATIO + 1
    c = x.reshape(B, ns, NSA_CMP_STRIDE, E)
    blocks = jnp.concatenate([c[:, j:j + nc] for j in range(NSA_CMP_RATIO)], axis=2)
    blocks = (blocks + pos_emb.astype(x.dtype)).reshape(B, nc, NSA_CMP_LEN * E)
    return jax.nn.gelu(blocks @ w1) @ w2

def nsa_compressed(q, k, v, pos_emb, w1, w2, slopes):
    B, T, H, E = q.shape
    kc = compress_blocks(k, pos_emb[0], w1[0], w2[0])
    vc = compress_blocks(v, pos_emb[1], w1[1], w2[1])
    nc = kc.shape[1]
    end = jnp.arange(nc) * NSA_CMP_STRIDE + NSA_CMP_LEN - 1
    dist = (jnp.arange(T)[:, None] - end[None, :]).astype(jnp.float32)
    s = (jnp.einsum('bthd,bnd->bhtn', q, kc).astype(jnp.float32) * (E ** -0.5)
         - slopes[:, None, None] * dist)
    p = masked_softmax(s, dist >= 0)
    return jnp.einsum('bhtn,bnd->bthd', p.astype(q.dtype), vc), p

def nsa_selected(q, k, v, p_cmp, slopes):
    B, T, H, E = q.shape
    nc = p_cmp.shape[-1]
    nsb = T // NSA_SEL_BLOCK
    n_sel = min(NSA_N_SEL, nsb)
    cs = np.arange(nc) * NSA_CMP_STRIDE
    bs = np.arange(nsb) * NSA_SEL_BLOCK
    inter = np.clip(np.minimum(cs[:, None] + NSA_CMP_LEN, bs[None, :] + NSA_SEL_BLOCK)
                    - np.maximum(cs[:, None], bs[None, :]), 0, None).astype(np.float32) / NSA_CMP_LEN
    imp = jnp.einsum('bhtn,nj->btj', p_cmp, jnp.asarray(inter))
    cur = jnp.arange(T)[:, None] // NSA_SEL_BLOCK
    blk = jnp.arange(nsb)[None, :]
    forced = (blk == 0) | (blk == cur) | (blk == cur - 1)
    score = jnp.where(blk <= cur, imp + jnp.where(forced, NSA_FORCE_BONUS, 0.0), NEG_INF)
    _, idx = lax.top_k(score, n_sel)

    kb = k.reshape(B, nsb, NSA_SEL_BLOCK, E)
    vb = v.reshape(B, nsb, NSA_SEL_BLOCK, E)
    QB = NSA_SEL_Q_BLOCK
    nqb = T // QB
    qs = jnp.moveaxis(q.reshape(B, nqb, QB, H, E), 1, 0)
    idxs = jnp.moveaxis(idx.reshape(B, nqb, QB, n_sel), 1, 0)
    t0s = jnp.arange(nqb) * QB
    bidx = jnp.arange(B)[:, None, None]

    def one_block(args):
        q_blk, idx_blk, t0 = args
        kg = kb[bidx, idx_blk]
        vg = vb[bidx, idx_blk]
        tq = t0 + jnp.arange(QB)
        pos = idx_blk[..., None] * NSA_SEL_BLOCK + jnp.arange(NSA_SEL_BLOCK)
        dist = (tq[None, :, None, None] - pos).astype(jnp.float32)[:, :, None]
        s = (jnp.einsum('bqhd,bqnsd->bqhns', q_blk, kg).astype(jnp.float32) * (E ** -0.5)
             - slopes[None, None, :, None, None] * dist)
        mask = jnp.broadcast_to(dist >= 0, s.shape)
        p = masked_softmax(s.reshape(B, QB, H, -1), mask.reshape(B, QB, H, -1)).reshape(s.shape)
        return jnp.einsum('bqhns,bqnsd->bqhd', p.astype(q_blk.dtype), vg)

    o = lax.map(one_block, (qs, idxs, t0s))
    return jnp.moveaxis(o, 0, 1).reshape(B, T, H, E)

def nsa_window(q, k, v, slopes):
    B, T, H, E = q.shape
    QB = NSA_Q_BLOCK
    nb = T // QB
    nprev = NSA_WINDOW // QB

    def band(t):
        tb = jnp.pad(t.reshape(B, nb, QB, E), ((0, 0), (nprev, 0), (0, 0), (0, 0)))
        return jnp.concatenate([tb[:, j:j + nb] for j in range(nprev + 1)], axis=2)

    kband, vband = band(k), band(v)
    qb = q.reshape(B, nb, QB, H, E)
    tq = jnp.arange(nb)[:, None] * QB + jnp.arange(QB)
    pos = jnp.arange(nb)[:, None] * QB - nprev * QB + jnp.arange((nprev + 1) * QB)
    dist = tq[:, :, None] - pos[:, None, :]
    mask = (dist >= 0) & (dist < NSA_WINDOW) & (pos[:, None, :] >= 0)
    s = (jnp.einsum('bnqhd,bnkd->bnhqk', qb, kband).astype(jnp.float32) * (E ** -0.5)
         - slopes[None, None, :, None, None] * dist.astype(jnp.float32)[None, :, None])
    p = masked_softmax(s, mask[None, :, None])
    o = jnp.einsum('bnhqk,bnkd->bnqhd', p.astype(q.dtype), vband)
    return o.reshape(B, T, H, E)

def native_sparse_attention(q, kv, gate_logit, z, cmp_pos, cmp_w1, cmp_w2):
    B, T, _ = q.shape
    q = q.reshape(B, T, N_HEADS, HEAD_DIM)
    k_c, v_c, k_s, v_s, k_w, v_w = jnp.split(kv, 6, axis=-1)
    slopes = jnp.asarray(ALIBI_SLOPES, jnp.float32)
    o_cmp, p_cmp = nsa_compressed(q, k_c, v_c, cmp_pos, cmp_w1, cmp_w2, slopes)
    o_sel = nsa_selected(q, k_s, v_s, p_cmp, slopes)
    o_win = nsa_window(q, k_w, v_w, slopes)
    g = jax.nn.sigmoid(gate_logit.reshape(B, T, N_HEADS, 3))
    o = g[..., 0:1] * o_cmp + g[..., 1:2] * o_sel + g[..., 2:3] * o_win
    return o.reshape(B, T, MIX_WIDTH) * jax.nn.silu(z)

def hybrid_layer(x, norm_gain, w_in, gdn_conv, gdn_a_log, gdn_dt_bias, gdn_norm,
                 sg_ln_gain, sg_ln_bias, sg_w_s, sg_b_s,
                 rw_mu, rw_w_up, rw_w0, rw_a_up, rw_a0, rw_k_k, rw_k_a, rw_r_k, rw_gn_gain, rw_gn_bias,
                 nsa_cmp_pos, nsa_cmp_w1, nsa_cmp_w2, w_branch, w_out):
    h = rmsnorm(x, norm_gain)
    proj = h @ w_in
    (gdn_qkv, gdn_a, gdn_b, gdn_z, sg_u, sg_v, sg_z, rw, rw_z,
     nsa_q, nsa_kv, nsa_g, nsa_z, merge) = jnp.split(proj, IN_OFFSETS, axis=-1)
    ys = (
        gated_deltanet(gdn_qkv, gdn_a, gdn_b, gdn_z, gdn_conv, gdn_a_log, gdn_dt_bias, gdn_norm),
        spatial_gating(sg_u, sg_v, sg_z, sg_ln_gain, sg_ln_bias, sg_w_s, sg_b_s),
        rwkv7_time_mix(rw, rw_z, rw_mu, rw_w_up, rw_w0, rw_a_up, rw_a0, rw_k_k, rw_k_a, rw_r_k,
                       rw_gn_gain, rw_gn_bias),
        native_sparse_attention(nsa_q, nsa_kv, nsa_g, nsa_z, nsa_cmp_pos, nsa_cmp_w1, nsa_cmp_w2),
    )
    gates = jnp.split(jax.nn.sigmoid(merge), N_MIXERS, axis=-1)
    mixed = gates[0] * (ys[0] @ w_branch[0])
    for i in range(1, N_MIXERS):
        mixed = mixed + gates[i] * (ys[i] @ w_branch[i])
    return x + mixed @ w_out

def second_inputs(seed: int = 0) -> dict:
    key = jax.random.key(seed)
    ks = jax.random.split(key, 32)
    f32 = jnp.float32
    L, D, W, H, E = DEPTH_2, D_MODEL, MIX_WIDTH, N_HEADS, HEAD_DIM
    nrm = lambda k, shape, scale: scale * jax.random.normal(k, shape, f32)
    dt = jnp.exp(jax.random.uniform(ks[5], (L, H), f32, math.log(1e-3), math.log(1e-1)))
    return {
        'x': nrm(ks[0], (BATCH, SEQ, D), 1.0),
        'norm_gain': 1.0 + nrm(ks[1], (L, D), 0.1),
        'w_in': nrm(ks[2], (L, D, D_IN), D ** -0.5),
        'gdn_conv': nrm(ks[3], (L, GDN_CONV, 3 * W), 0.5),
        'gdn_a_log': jnp.log(jax.random.uniform(ks[4], (L, H), f32, 1.0, 16.0)),
        'gdn_dt_bias': jnp.log(jnp.expm1(dt)),
        'gdn_norm': 1.0 + nrm(ks[6], (L, E), 0.1),
        'sg_ln_gain': 1.0 + nrm(ks[7], (L, W), 0.1),
        'sg_ln_bias': nrm(ks[8], (L, W), 0.02),
        'sg_w_s': nrm(ks[9], (L, SG_GROUPS, SG_CHUNK, SG_CHUNK), SG_CHUNK ** -0.5),
        'sg_b_s': 1.0 + nrm(ks[10], (L, SG_GROUPS, SG_CHUNK), 0.1),
        'rw_mu': jax.random.uniform(ks[11], (L, RW_WIDTH), f32, 0.0, 1.0),
        'rw_w_up': nrm(ks[12], (L, RWKV_DECAY_RANK, W), 0.1),
        'rw_w0': jax.random.uniform(ks[13], (L, W), f32, -6.0, -1.0),
        'rw_a_up': nrm(ks[14], (L, RWKV_A_RANK, W), 0.1),
        'rw_a0': nrm(ks[15], (L, W), 0.1),
        'rw_k_k': 0.85 + nrm(ks[16], (L, W), 0.05),
        'rw_k_a': 1.0 + nrm(ks[17], (L, W), 0.05),
        'rw_r_k': nrm(ks[18], (L, H, E), 0.1),
        'rw_gn_gain': 1.0 + nrm(ks[19], (L, W), 0.1),
        'rw_gn_bias': nrm(ks[20], (L, W), 0.02),
        'nsa_cmp_pos': nrm(ks[21], (L, 2, NSA_CMP_LEN, NSA_KV_DIM), 0.1),
        'nsa_cmp_w1': nrm(ks[22], (L, 2, NSA_CMP_LEN * NSA_KV_DIM, NSA_CMP_HIDDEN), (NSA_CMP_LEN * NSA_KV_DIM) ** -0.5),
        'nsa_cmp_w2': nrm(ks[23], (L, 2, NSA_CMP_HIDDEN, NSA_KV_DIM), NSA_CMP_HIDDEN ** -0.5),
        'w_branch': nrm(ks[24], (L, N_MIXERS, W, D), W ** -0.5),
        'w_out': nrm(ks[25], (L, D, D), D ** -0.5),
        'final_gain': 1.0 + nrm(ks[26], (D,), 0.1),
    }

def second_block(x, norm_gain, w_in, gdn_conv, gdn_a_log, gdn_dt_bias, gdn_norm,
              sg_ln_gain, sg_ln_bias, sg_w_s, sg_b_s,
              rw_mu, rw_w_up, rw_w0, rw_a_up, rw_a0, rw_k_k, rw_k_a, rw_r_k, rw_gn_gain, rw_gn_bias,
              nsa_cmp_pos, nsa_cmp_w1, nsa_cmp_w2, w_branch, w_out, final_gain):
    for l in range(DEPTH_2):
        x = hybrid_layer(
            x, norm_gain[l], w_in[l], gdn_conv[l], gdn_a_log[l], gdn_dt_bias[l], gdn_norm[l],
            sg_ln_gain[l], sg_ln_bias[l], sg_w_s[l], sg_b_s[l],
            rw_mu[l], rw_w_up[l], rw_w0[l], rw_a_up[l], rw_a0[l], rw_k_k[l], rw_k_a[l], rw_r_k[l],
            rw_gn_gain[l], rw_gn_bias[l],
            nsa_cmp_pos[l], nsa_cmp_w1[l], nsa_cmp_w2[l], w_branch[l], w_out[l])
    return rmsnorm(x, final_gain)


def setup_inputs(seed=0):
    out = dict(first_inputs(seed))
    for name, value in second_inputs(seed + 1).items():
        if name != "x":
            out[name + "_2"] = value
    return out


def reference(
    x, pre_mix_g, post_mix_g, pre_ffn_g, post_ffn_g, ab_w_in, ab_b_in, conf_conv_w, conf_conv_b,
    conf_ln_g, conf_ln_b, lru_conv_w, lru_conv_b, lru_w_a, lru_b_a, lru_w_x, lru_b_x,
    lru_lambda, ab_w_out, ml_w_in, ml_b_in, ml_head_g, ml_w_out, ffn_w_gate, ffn_w_up,
    ffn_w_down, norm_gain_2, w_in_2, gdn_conv_2, gdn_a_log_2, gdn_dt_bias_2, gdn_norm_2,
    sg_ln_gain_2, sg_ln_bias_2, sg_w_s_2, sg_b_s_2, rw_mu_2, rw_w_up_2, rw_w0_2, rw_a_up_2,
    rw_a0_2, rw_k_k_2, rw_k_a_2, rw_r_k_2, rw_gn_gain_2, rw_gn_bias_2, nsa_cmp_pos_2,
    nsa_cmp_w1_2, nsa_cmp_w2_2, w_branch_2, w_out_2, final_gain_2,
):
    x = first_block(
        x, pre_mix_g, post_mix_g, pre_ffn_g, post_ffn_g, ab_w_in, ab_b_in, conf_conv_w,
        conf_conv_b, conf_ln_g, conf_ln_b, lru_conv_w, lru_conv_b, lru_w_a, lru_b_a, lru_w_x,
        lru_b_x, lru_lambda, ab_w_out, ml_w_in, ml_b_in, ml_head_g, ml_w_out, ffn_w_gate,
        ffn_w_up, ffn_w_down,
    )
    return second_block(
        x, norm_gain_2, w_in_2, gdn_conv_2, gdn_a_log_2, gdn_dt_bias_2, gdn_norm_2,
        sg_ln_gain_2, sg_ln_bias_2, sg_w_s_2, sg_b_s_2, rw_mu_2, rw_w_up_2, rw_w0_2, rw_a_up_2,
        rw_a0_2, rw_k_k_2, rw_k_a_2, rw_r_k_2, rw_gn_gain_2, rw_gn_bias_2, nsa_cmp_pos_2,
        nsa_cmp_w1_2, nsa_cmp_w2_2, w_branch_2, w_out_2, final_gain_2,
    )


_drawn_inputs = setup_inputs


def setup_inputs(seed=0):
    import zlib

    import numpy as np

    out = dict(_drawn_inputs(seed))
    spreads = {}
    factors = {'lru_b_a': 8.0,
     'lru_b_x': 8.0,
     'gdn_norm_2': 4.309,
     'sg_ln_gain_2': 8.0,
     'sg_ln_bias_2': 64.0,
     'sg_b_s_2': 5.863,
     'rw_w_up_2': 7.49,
     'rw_a0_2': 8.0,
     'rw_k_k_2': 33.507,
     'rw_k_a_2': 6.769,
     'rw_gn_gain_2': 4.356,
     'rw_gn_bias_2': 30.723,
     'nsa_cmp_pos_2': 8.0}
    for name, (base, spread) in spreads.items():
        noise = np.random.default_rng([zlib.crc32(name.encode()), seed]).standard_normal(out[name].shape)
        drawn = base * np.exp(spread * noise) if base else spread * noise
        out[name] = jnp.asarray(drawn.astype(out[name].dtype))
    for name, factor in factors.items():
        out[name] = (out[name] * factor).astype(out[name].dtype)
    return out
```

```python
from contextlib import ExitStack

import numpy as np

from concourse import mybir

F32 = mybir.dt.float32
F32R = mybir.dt.float32r
ALU = mybir.AluOpType
ACT = mybir.ActivationFunctionType
AX = mybir.AxisListType.X
MUL, ADD, SUB, MAX, MIN = ALU.mult, ALU.add, ALU.subtract, ALU.max, ALU.min

T = 1024
D = 1024
EPS = 1e-6
FF = 2816
FG = [3, 3, 3, 3, 3, 3, 2, 2]
NSPLIT = 2
NRAW = 3


class Scope(ExitStack):

    def __init__(self, side="left"):
        super().__init__()
        self.side = side


class Engine:

    def __init__(self, name, sem, serial):
        self.name, self.sem, self.serial = name, sem, serial
        self.queue, self.count, self.seen = [], 0, {}

    def wait(self, after):
        for sem, value in after:
            if self.seen.get(id(sem), 0) < value:
                self.seen[id(sem)] = value
                self.queue.append((None, sem, value))

    def put(self, fn, after=(), inc=True, free=False):
        if self.serial and not free and self.count:
            self.wait([(self.sem, self.count)])
        self.wait(after)
        self.queue.append((fn, self.sem if inc else None, 1))
        if inc:
            self.count += 1
        return (self.sem, self.count)

    def load(self, fn, sem, value, after=()):
        self.wait(after)
        self.queue.append((fn, sem, 16))
        return (sem, value)

    def now(self):
        return (self.sem, self.count)

    def emit(self, eng):
        for fn, sem, value in self.queue:
            if fn is None:
                eng.wait_ge(sem, value)
            elif sem is None:
                fn(eng)
            else:
                fn(eng).then_inc(sem, value)


class Machine:
    def __init__(self, nc, ctx):
        self.nc, self.ctx = nc, ctx
        sem = lambda n: ctx.enter_context(nc.semaphore(n))
        self.newsem = sem
        self.T = Engine("tensor", sem("s_tensor"), False)
        self.V = Engine("vector", sem("s_vector"), True)
        self.S = Engine("scalar", sem("s_scalar"), True)
        self.G = Engine("gpsimd", sem("s_gpsimd"), True)
        self.Y = Engine("sync", sem("s_sync"), False)
        self.names = 0

    def sb(self, shape, dt=F32, ctx=None, name="t"):
        self.names += 1
        ctx = ctx or self.ctx
        return ctx.enter_context(self.nc.sbuf_tensor(f"{name}_{self.names}", shape, dt, side=ctx.side))

    def fence(self):
        now = [e.now() for e in (self.T, self.V, self.S, self.G)]
        for e in (self.V, self.S, self.G):
            e.wait([t for t in now if t[1]])
        return [t for t in now if t[1]]

    def mm(self, out, lhsT, rhs, start, stop, after=(), inc=False):
        return self.T.put(lambda e: e.matmul(out, lhsT, rhs, start=start, stop=stop, skip_group_check=True), after, inc)

    def tr(self, out, in_, ident, after=(), inc=False):
        return self.T.put(lambda e: e.transpose(out, in_, ident), after, inc)

    def act(self, out, in_, func, after=(), bias=None, scale=1.0, accum=None, free=False):
        kw = {"scale": scale}
        if bias is not None:
            kw["bias"] = bias
        if accum is not None:
            kw["accum_out"] = accum
        return self.S.put(lambda e: e.activation(out, in_, func, **kw), after, free=free)

    def tt(self, out, a, b, op, after=(), eng=None, free=False):
        return (eng or self.V).put(lambda e: e.tensor_tensor(out, a, b, op), after, free=free)

    def ts(self, out, a, s1, op0, s2=None, op1=None, after=(), eng=None, free=False):
        if op1 is None:
            return (eng or self.V).put(lambda e: e.tensor_scalar(out, a, s1, None, op0), after, free=free)
        return (eng or self.V).put(lambda e: e.tensor_scalar(out, a, s1, s2, op0, op1), after, free=free)

    def stt(self, out, a, s, b, op0, op1, after=(), eng=None, free=False):
        return (eng or self.V).put(lambda e: e.scalar_tensor_tensor(out=out, in0=a, scalar=s, in1=b, op0=op0, op1=op1), after, free=free)

    def cp(self, out, a, after=(), eng=None, free=False):
        return (eng or self.V).put(lambda e: e.tensor_copy(out, a), after, free=free)

    def scan(self, out, a, b, init, op0, op1, after=()):
        return self.V.put(lambda e: e.tensor_tensor_scan(out, a, b, init, op0, op1), after)

    def recip(self, out, a, after=(), free=False):
        return self.V.put(lambda e: e.reciprocal(out, a), after, free=free)

    def fill(self, out, v, after=(), eng=None):
        return (eng or self.V).put(lambda e: e.memset(out, v), after)


class Banks:

    def __init__(self, tensor, units):
        self.t, self.idle = tensor, list(units)
        self.unit = len(units[0])
        self.free = {tuple(b): [] for b in units}

    def take(self, k=1):
        assert k == self.unit
        got = self.idle.pop(0)
        return list(got), self.free[tuple(got)]

    def give(self, got, readers):
        self.free[tuple(got)] = list(readers)
        self.idle.append(got)


class Weights:

    def __init__(self, M, dram):
        self.M, self.dram = M, dram
        self.n = dram.shape[0]
        self.order = []
        self.raw = M.sb([128, NRAW, 1024], name="wraw")
        self.hi = M.sb([128, NSPLIT, 1024], F32R, name="whi")
        self.lo = M.sb([128, NSPLIT, 1024], F32R, name="wlo")
        self.sems = [M.newsem(f"s_w{i}") for i in range(NRAW)]
        self.loaded, self.split, self.block = 0, 0, 0
        self.ready, self.used, self.rawfree, self.arrived = {}, {}, {}, {}
        for _ in range(NRAW):
            self.load()

    def load(self):
        c = self.loaded
        if c >= self.n:
            return
        s = c % NRAW
        dst, src = self.raw[:, s, :], self.dram[c]
        self.arrived[c] = self.M.Y.load(lambda e: e.dma_start(dst, src), self.sems[s], 16 * (c // NRAW + 1),
                                        after=self.rawfree.get(c - NRAW, []))
        self.loaded += 1

    def make(self, c):
        while self.split <= min(c, self.n - 1):
            n, M = self.split, self.M
            r, s = n % NRAW, n % NSPLIT
            gone = self.used.get(n - NSPLIT, [])
            a = M.act(self.hi[:, s, :], self.raw[:, r, :], ACT.Copy, after=[self.arrived[n], *gone])
            b = M.tt(self.lo[:, s, :], self.raw[:, r, :], self.hi[:, s, :].bitcast(F32), SUB, after=[a, *gone], eng=M.G)
            self.ready[n] = [a, b]
            self.rawfree[n] = [a, b]
            self.split += 1
            self.load()

    def get(self, k, src):
        out, chunks = [], set()
        for _ in range(k):
            self.order.append(src)
            c, o = divmod(self.block, 8)
            self.make(c)
            sl = slice(o * 128, o * 128 + 128)
            out.append((self.hi[:, c % NSPLIT, sl], self.lo[:, c % NSPLIT, sl], self.ready[c]))
            chunks.add(c)
            self.block += 1
        return out, chunks

    def done(self, chunks, token):
        for c in chunks:
            self.used[c] = [token]
        self.make(self.block // 8 + 1)


class Split:

    def __init__(self, M, k, ctx):
        self.hi = M.sb([128, k, T], F32R, ctx, "xhi")
        self.lo = M.sb([128, k, T], F32R, ctx, "xlo")
        self.k, self.w = k, [[] for _ in range(k)]

    def store(self, M, i, src, after=(), eng=None):
        a = M.act(self.hi[:, i, :], src, ACT.Copy, after=after)
        b = M.tt(self.lo[:, i, :], src, self.hi[:, i, :].bitcast(F32), SUB, after=[a, *after], eng=eng)
        self.w[i] = [a, b]
        return [a, b]


def run(gen):
    for _ in gen:
        pass


def side_by_side(one, steps_one, other, steps_other):
    live = [[one, steps_one, 0], [other, steps_other, 0]]
    while live:
        g = min(live, key=lambda x: x[2] / x[1])
        g[2] += 1
        if next(g[0], StopIteration) is StopIteration:
            live.remove(g)


def dense(M, W, P, ks, m_tiles, evac, src="main"):
    for m in range(m_tiles):
        blocks, chunks = W.get(len(ks), src)
        got, free = P.take(2)
        ps = P.t[:, got[0]:got[0] + 2, :]
        n = len(ks)
        for i, ((whi, wlo, ready), (xhi, xlo, xw)) in enumerate(zip(blocks, ks)):
            for j, (w, x) in enumerate(((whi, xhi), (whi, xlo), (wlo, xhi))):
                for h in range(2):
                    tok = M.mm(ps[:, h, :], w, x[:, h * 512:(h + 1) * 512], start=(i == 0 and j == 0),
                               stop=(i == n - 1 and j == 2), after=[*free, *ready, *xw], inc=(i == n - 1 and j == 2 and h == 1))
            if i < n - 1:
                yield None
        W.done(chunks, tok)
        P.give(got, evac(m, ps, tok))
        yield m


def rstd_rows(M, P, C, src, k, width, after, out, sq, centred=None):
    toks = []
    got, free = P.take(2)
    ps = P.t[:, got[0]:got[0] + 2, :]
    prev = [[], []]
    for i in range(k):
        a = M.act(sq[:, i % 2, :], src(i), ACT.Square, after=[*after[i], *prev[i % 2]])
        for h in range(2):
            t = M.mm(ps[:, h, :], C.ones[:, :], sq[:, i % 2, h * 512:(h + 1) * 512], start=(i == 0), stop=(i == k - 1),
                     after=[*free, a], inc=(h == 1))
        prev[i % 2] = [t]
    a = M.act(out, ps, ACT.Sqrt, after=[t], bias=C.eps[:, 0:1], scale=1.0 / width)
    P.give(got, [a])
    return M.recip(out, out, after=[a])


class Consts:
    pass


class Residual:

    def __init__(self, M, dram, keep):
        self.M, self.dram, self.keep = M, dram, keep
        self.sem, self.n = M.newsem("s_x"), 0
        self.w, self.stored = [[] for _ in range(8)], []

    def load(self):
        self.ctx = Scope()
        self.t = self.M.sb([128, 8, T], ctx=self.ctx, name="x")
        t, src = self.t, self.dram
        self.n += 16
        tok = self.M.Y.load(lambda e: e.dma_start(t[:, :, :], src), self.sem, self.n, after=[*self.stored, *self.M.fence()])
        self.w = [[tok] for _ in range(8)]

    def set_aside(self):
        self.dram = self.keep
        t, dst = self.t, self.keep
        self.n += 16
        self.stored = [self.M.Y.load(lambda e: e.dma_start(dst, t[:, :, :]), self.sem, self.n, after=[x for w in self.w for x in w])]
        for e in (self.M.T, self.M.V, self.M.S, self.M.G):
            e.wait(self.stored)
        self.ctx.close()


def norm_split(M, P, C, X, xw, g, Hs):
    with Scope('right') as c:
        sq = M.sb([128, 2, T], ctx=c)
        rs = M.sb([128, T], ctx=c)
        tmp = M.sb([128, 2, T], ctx=c)
        r = rstd_rows(M, P, C, lambda i: X[:, i, :], 8, D, xw, rs[:, :], sq)
        last = [[], []]
        for i in range(8):
            t = M.stt(tmp[:, i % 2, :], X[:, i, :], g(i), rs[:, :], MUL, MUL, after=[r, *last[i % 2]])
            last[i % 2] = Hs.store(M, i, tmp[:, i % 2, :], [t], eng=(M.V if i % 2 else M.G))
        M.fence()


def add_normed(M, P, C, X, xw, Y, yw, g):
    with Scope() as c:
        sq = M.sb([128, 2, T], ctx=c)
        rs = M.sb([128, T], ctx=c)
        r = rstd_rows(M, P, C, lambda i: Y[:, i, :], 8, D, yw, rs[:, :], sq)
        out = []
        for i in range(8):
            t = M.stt(Y[:, i, :], Y[:, i, :], g(i), rs[:, :], MUL, MUL, after=[r])
            out.append([M.tt(X[:, i, :], X[:, i, :], Y[:, i, :], ADD, after=[t, *xw[i]], eng=(M.V if i % 2 else M.G))])
        M.fence()
    return out


def ffn(M, W, P, C, R, g_pre, g_post):
    X, xw = R.t, R.w
    with Scope() as c:
        acc = M.sb([128, 8, T], ctx=c, name="acc")
        accw = [[] for _ in range(8)]
        with Scope('right') as c2:
            H = Split(M, 8, c2)
            norm_split(M, P, C, X, xw, g_pre, H)
            ks = [(H.hi[:, i, :], H.lo[:, i, :], H.w[i]) for i in range(8)]
            NA = 4
            A = Split(M, NA, c2)
            sil = M.sb([128, T], ctx=c2)
            afree = [[] for _ in range(NA)]
            state = {"n": 0}

            def gate_up():
                j = state["n"] % NA
                state["n"] += 1
                hold = {}

                def evac(m, ps, tok):
                    if m == 0:
                        hold["s"] = M.act(sil[:, :], ps, ACT.Silu, after=[tok, *hold.get("u", [])])
                        return [hold["s"]]
                    u = M.tt(sil[:, :], sil[:, :], ps, MUL, after=[tok, hold["s"]])
                    A.store(M, j, sil[:, :], [u, *afree[j]], eng=M.V)
                    return [u]
                hold["u"] = A.w[(j - 1) % NA]
                run(dense(M, W, P, ks, 2, evac))
                return j

            def down(slots, first):
                def evac(m, ps, tok):
                    if first:
                        t = M.act(acc[:, m, :], ps, ACT.Copy, after=[tok])
                    else:
                        t = M.tt(acc[:, m, :], acc[:, m, :], ps, ADD, after=[tok, *accw[m]])
                    accw[m] = [t]
                    return [t]
                run(dense(M, W, P, [(A.hi[:, j, :], A.lo[:, j, :], A.w[j]) for j in slots], 8, evac))
                for j in slots:
                    afree[j] = [M.T.now()]

            slots = [gate_up() for _ in range(FG[0])]
            for n, size in enumerate(FG):
                nxt = []
                if n + 1 < len(FG):
                    nxt.append(gate_up())
                down(slots, n == 0)
                slots = nxt
                if n + 1 < len(FG):
                    slots += [gate_up() for _ in range(FG[n + 1] - 1)]
            M.fence()
        R.w = add_normed(M, P, C, X, xw, acc, accw, g_post)


def conv(M, dst, src, w, b, taps, after, eng=None):
    t = M.ts(dst, src[:, 0:T], w[:, 0:1], MUL, b, ADD, after=after, eng=eng) if b is not None else \
        M.ts(dst, src[:, 0:T], w[:, 0:1], MUL, after=after, eng=eng)
    for k in range(1, taps):
        t = M.stt(dst, src[:, k:k + T], w[:, k:k + 1], dst, MUL, ADD, after=[t], eng=eng)
    return t


def softplus_neg(M, x, tmp, after):
    y, s, z, p = tmp
    a = M.act(y, x, ACT.Abs, after=after)
    a = M.act(y, y, ACT.Exp, after=[a], scale=-1.0)
    v = M.ts(s, y, 2.0, ADD, after=[a])
    v = M.recip(s, s, after=[v])
    v = M.tt(s, s, y, MUL, after=[v])
    v = M.tt(z, s, s, MUL, after=[v])
    v = M.ts(p, z, 2.0 / 15, MUL, 2.0 / 13, ADD, after=[v])
    for c in (11, 9, 7, 5, 3, 1):
        v = M.tt(p, p, z, MUL, after=[v])
        v = M.ts(p, p, 2.0 / c, ADD, after=[v])
    v = M.tt(p, p, s, MUL, after=[v])
    v = M.ts(x, x, -1.0, MUL, 0.0, MAX, after=[v])
    return M.tt(x, x, p, ADD, after=[v])


def mixer0(M, W, P, C, A, X, pv):
    c2 = Scope("right")
    H = Split(M, 8, c2)
    norm_split(M, P, C, X.t, X.w, lambda i: pv("pre_mix_g0", i), H)
    X.set_aside()
    c = Scope()
    GI = M.sb([128, 4, T], ctx=c, name="gi")
    CA = M.sb([128, 4, T], ctx=c, name="ca")
    c1 = Scope()
    Yc = M.sb([128, 4, 30 + T], ctx=c1, name="yc")
    RI = M.sb([128, 4, 3 + T], ctx=c1, name="ri")
    lru_w = M.sb([128, 2, 4, 128], ctx=c1, name="lru")
    wld = M.Y.load(lambda e: e.dma_start(lru_w[:, :, :, :], A["lru"]), M.newsem("s_lru"), 16, after=[*M.fence(), *X.stored])
    z = [M.fill(Yc[:, :, 0:30], 0.0), M.fill(RI[:, :, 0:3], 0.0)]
    yw, rw, gw, hold = {}, {}, {}, {}
    with c2:
        tmp = M.sb([128, 2, T], ctx=c2)
        ks = [(H.hi[:, i, :], H.lo[:, i, :], H.w[i]) for i in range(8)]

        def evac(m, ps, tok):
            if m < 8:
                j = m // 2
                if m % 2 == 0:
                    hold["v"] = M.act(Yc[:, j, 30:], ps, ACT.Identity, after=[tok], bias=pv("ab_b_in", j))
                    return [hold["v"]]
                t = M.act(tmp[:, j % 2, :], ps, ACT.Sigmoid, after=[tok, *hold.get(j % 2, [])], bias=pv("ab_b_in", 4 + j))
                u = M.tt(Yc[:, j, 30:], Yc[:, j, 30:], tmp[:, j % 2, :], MUL, after=[t, hold["v"]], eng=M.V)
                hold[j % 2] = [u]
                yw[j] = [u, z[0]]
                return [t]
            j = m % 4
            if m < 12:
                t = M.act(RI[:, j, 3:], ps, ACT.Identity, after=[tok], bias=pv("ab_b_in", 12 + j))
                rw[j] = [t, z[1]]
                return [t]
            t = M.act(GI[:, j, :], ps, ACT.Gelu_apprx_tanh, after=[tok], bias=pv("ab_b_in", 8 + j))
            gw[j] = [t]
            return [t]
        ct = {}
        for m in dense(M, W, P, ks, 16, evac):
            if m is not None and m < 8 and m % 2:
                j = m // 2
                ct[j] = [conv(M, CA[:, j, :], Yc[:, j, :], C.cols("conf_conv_w", j), pv("conf_conv_b", j), 31, yw[j])]
        M.fence()
    sp = M.sb([128, 4], ctx=c1)
    spt = M.sb([128, 4, 4], ctx=c1)
    neg = M.sb([128, 4], ctx=c1)
    t = M.cp(sp[:, :], C.span("lru_lambda"), after=C.ready)
    t = softplus_neg(M, sp[:, :], [spt[:, i, :] for i in range(4)], [t])
    t = M.ts(sp[:, :], sp[:, :], 8.0, MUL, after=[t])
    spw = M.ts(neg[:, :], sp[:, :], -1.0, MUL, after=[t])
    XR, a_, r_, t_, i_ = (M.sb([128, T], ctx=c1) for _ in range(5))
    last, lw = [], {}
    for j in range(4):
        t = conv(M, XR[:, :], RI[:, j, :], C.cols("lru_conv_w", j), pv("lru_conv_b", j), 4, [*rw[j], *last])
        res = []
        for wi, (dst, bn) in enumerate(((r_, "lru_b_a"), (i_, "lru_b_x"))):
            got, free = P.take(2)
            ps = P.t[:, got[0]:got[0] + 2, :]
            for h in range(2):
                m = M.mm(ps[:, h, :], lru_w[:, wi, j, :], XR[:, h * 512:(h + 1) * 512], True, True,
                         after=[*free, t, wld], inc=True)
            s = M.act(dst[:, :], ps, ACT.Sigmoid, after=[m, *last], bias=pv(bn, j))
            P.give(got, [s])
            res.append(s)
        e = M.act(a_[:, :], r_[:, :], ACT.Exp, after=[res[0], spw], scale=neg[:, j:j + 1])
        t = M.act(t_[:, :], r_[:, :], ACT.Tanh, after=[e], scale=sp[:, j:j + 1])
        u = M.ts(r_[:, :], t_[:, :], 1.0, ADD, after=[t])
        u = M.recip(r_[:, :], r_[:, :], after=[u])
        u = M.tt(r_[:, :], r_[:, :], t_[:, :], MUL, after=[u])
        q = M.act(r_[:, :], r_[:, :], ACT.Sqrt, after=[u], scale=2.0)
        u = M.tt(i_[:, :], i_[:, :], XR[:, :], MUL, after=[res[1]])
        u = M.tt(i_[:, :], i_[:, :], r_[:, :], MUL, after=[q, u])
        u = M.scan(t_[:, :], a_[:, :], i_[:, :], 0.0, MUL, ADD, after=[u, e])
        u = M.tt(GI[:, j, :], t_[:, :], GI[:, j, :], MUL, after=[u, *gw[j]])
        last, lw[j] = [u], [u]
    got, free = P.take(2)
    ps = P.t[:, got[0]:got[0] + 2, :]
    for j in range(4):
        for h in range(2):
            m = M.mm(ps[:, h, :], C.ones[:, :], CA[:, j, h * 512:(h + 1) * 512], j == 0, j == 3, after=[*free, *ct[j]],
                     inc=(h == 1))
    mu = M.act(t_[:, :], ps, ACT.Copy, after=[m, *last], scale=1.0 / 512)
    P.give(got, [mu])
    cent = [[M.tt(CA[:, j, :], CA[:, j, :], t_[:, :], SUB, after=[mu, m], eng=M.V if j % 2 else M.G)] for j in range(4)]
    with Scope() as c4:
        sq = M.sb([128, 2, T], ctx=c4)
        r = rstd_rows(M, P, C, lambda i: CA[:, i, :], 4, 512, cent, r_[:, :], sq)
        cw = {}
        for j in range(4):
            t = M.stt(CA[:, j, :], CA[:, j, :], pv("conf_ln_g", j), r_[:, :], MUL, MUL, after=[r])
            cw[j] = [M.act(CA[:, j, :], CA[:, j, :], ACT.Silu, after=[t], bias=pv("conf_ln_b", j))]
        M.fence()
    c1.close()
    Yt = {**{j: CA[:, j, :] for j in range(4)}, **{4 + j: GI[:, j, :] for j in range(4)}}
    g = mix_out(M, W, P, C, X, Yt, {**cw, **{4 + j: lw[j] for j in range(4)}}, lambda i: pv("post_mix_g0", i))
    next(g)
    c.close()
    run(g)


def mix_out(M, W, P, C, X, Y, yw, g):
    with Scope("right") as c2:
        YS = Split(M, 8, c2)
        for j in range(8):
            YS.store(M, j, Y[j], yw[j], eng=M.V if j % 2 else M.G)
        ks = [(YS.hi[:, i, :], YS.lo[:, i, :], YS.w[i]) for i in range(8)]
        O = M.sb([128, 8, T], ctx=c2, name="o")
        ow = {}

        def evac(m, ps, tok):
            ow[m] = [M.act(O[:, m, :], ps, ACT.Copy, after=[tok])]
            return ow[m]
        run(dense(M, W, P, ks, 8, evac))
        yield
        X.load()
        X.w = add_normed(M, P, C, X.t, X.w, O, ow, g)


def mixer1(M, W, P, Q, C, X, pv):
    c2 = Scope("right")
    H = Split(M, 8, c2)
    norm_split(M, P, C, X.t, X.w, lambda i: pv("pre_mix_g1", i), H)
    X.set_aside()
    hk = [(H.hi[:, i, :], H.lo[:, i, :], H.w[i]) for i in range(8)]
    c = Scope()
    Y = M.sb([128, 8, T], ctx=c, name="y")
    yw = {i: [] for i in range(8)}
    c1 = Scope()
    R = M.sb([40, T], ctx=c1, name="rows")
    gT = M.sb([128, 8, 8], ctx=c1, name="gt")
    with Scope() as ct:
        ig, fg, a1, a2, a3, a4 = (M.sb([8, T], ctx=ct) for _ in range(6))
        got = {}

        def evac(m, ps, tok):
            a = M.act(ig[:, :], ps[0:8], ACT.Identity, after=[tok], bias=C.ml_bi)
            b = M.act(R[32:40, :], ps[32:40], ACT.Identity, after=[tok], bias=C.ml_bf)
            got["t"] = [a, M.cp(fg[:, :], R[32:40, :], after=[b])]
            return [a, b]
        run(dense(M, W, P, hk, 1, evac))
        t = softplus_neg(M, fg[:, :], [x[:, :] for x in (a1, a2, a3, a4)], got["t"])
        z = M.fill(a1[:, :], 0.0, after=[t])
        t = M.scan(a2[:, :], fg[:, :], a1[:, :], 0.0, ADD, ADD, after=[t, z])
        t = M.tt(ig[:, :], ig[:, :], a2[:, :], ADD, after=[t])
        m = M.scan(a3[:, :], ig[:, :], ig[:, :], 0.0, MAX, MAX, after=[t])
        r0 = M.ts(R[0:8, :], a3[:, :], -1.0, MUL, after=[m])
        d = M.tt(a2[:, :], a2[:, :], a3[:, :], SUB, after=[m])
        r1 = M.act(R[32:40, :], a2[:, :], ACT.Exp, after=[d])
        b, free = Q.take(1)
        for i in range(8):
            tk = M.tr(Q.t[:, b[0], i * 8:(i + 1) * 8], ig[:, i * 128:(i + 1) * 128], C.ident[0:8, 0:8], after=[t, *free, *C.ready], inc=(i == 7))
        gw = M.cp(gT[:, :, :], Q.t[:, b[0], 0:64].rearrange("p (a b) -> p a b", a=8), after=[tk])
        Q.give(b, [gw])
        rows = [r0, r1, gw]
        M.fence()
    QK = M.sb([128, 2, 2, T], ctx=c1, name="qk")
    VT = M.sb([128, 2, 8, 256], ctx=c1, name="vt")
    VF = M.sb([128, T], ctx=c1, name="vf")
    BC = M.sb([128, 2, T], ctx=c1, name="bc")
    EX = M.sb([128, 2, 512], ctx=c1, name="ex")
    PP = M.sb([128, 2, 512], ctx=c1, name="pp")
    hh = M.sb([128, 512], ctx=c1, name="hh")
    dd = M.sb([128, 512], ctx=c1, name="dd")
    inw = {}
    use = {0: [], 1: []}

    def project(j):
        b = j % 2
        hold = {"v": []}

        def evac(m, ps, tok):
            if m == 0:
                t = M.act(QK[:, b, 0, :], ps, ACT.Identity, after=[tok, *use[b]], bias=pv("ml_b_in", j))
                inw[j] = [t]
                return [t]
            if m == 1:
                t = M.ts(QK[:, b, 1, :], ps, pv("ml_b_in", 4 + j), ADD, 0.125, MUL, after=[tok, *use[b]])
                inw[j].append(t)
                return [t]
            v = m - 2
            t = M.act(VF[:, :], ps, ACT.Identity, after=[tok, *hold["v"]], bias=pv("ml_b_in", 8 + 2 * j + v))
            for q in range(2):
                bk, free = Q.take(1)
                for i in range(4):
                    tk = M.tr(Q.t[:, bk[0], i * 128:(i + 1) * 128], VF[:, (4 * q + i) * 128:(4 * q + i + 1) * 128], C.ident[:, :],
                              after=[t, *free], inc=(i == 3))
                u = M.cp(VT[:, b, 4 * q:4 * q + 4, v * 128:(v + 1) * 128], Q.t[:, bk[0], :].rearrange("p (a b) -> p a b", a=4),
                         after=[tk, *use[b]])
                Q.give(bk, [u])
                inw[j].append(u)
            hold["v"] = [tk]
            return [t]
        yield from dense(M, W, P, hk, 4, evac)

    def heads(j):
        b = j % 2
        for s in range(2):
            h = 2 * j + s
            p0 = 64 * s
            bw = []
            for r in range(2):
                for hf in range(2):
                    bk, free = Q.take(1)
                    t = M.mm(Q.t[:, bk[0], :], C.sel[32 * r:32 * r + 8, h, :], R[32 * r:32 * r + 8, hf * 512:(hf + 1) * 512], True, True,
                             after=[*free, *rows], inc=True)
                    u = M.act(BC[:, r, hf * 512:(hf + 1) * 512], Q.t[:, bk[0], :], ACT.Copy, after=[t, *use.get("bc", [])])
                    Q.give(bk, [u])
                    bw.append(u)
            yield
            for hf in range(2):
                acc, afree = [], []
                for _ in range(2):
                    bk, free = Q.take(1)
                    acc += bk
                    afree += free
                items = list(range(4 * hf + 4))

                def score(i):
                    t0 = max(128 * i, 512 * hf)
                    o = t0 - 512 * hf
                    bk, free = Q.take(1)
                    sc = Q.t[:, bk[0], o:512]
                    t = M.mm(sc, QK[p0:p0 + 64, b, 1, i * 128:(i + 1) * 128], QK[p0:p0 + 64, b, 0, t0:512 * hf + 512], True, True,
                             after=[*free, *inw[j]], inc=True)
                    e = EX[:, i % 2, o:512]
                    prior = use.get(("p", i % 2), [])
                    g = gT[:, i, h:h + 1]
                    if 128 * i >= 512 * hf:
                        a = M.ts(EX[:, i % 2, o:o + 128], BC[:, 0, t0:t0 + 128], g, ADD, 0.0, MIN, after=[*bw, *rows, *prior])
                        a = M.act(EX[:, i % 2, o:o + 128], EX[:, i % 2, o:o + 128], ACT.Exp, after=[a])
                        x = M.tt(EX[:, i % 2, o:o + 128], EX[:, i % 2, o:o + 128], C.upper[:, :], MUL, after=[a], eng=M.G)
                        if o + 128 < 512:
                            a = M.act(EX[:, i % 2, o + 128:512], BC[:, 0, t0 + 128:512 * hf + 512], ACT.Exp, bias=g, after=[*bw, *prior])
                        w = [a, x]
                    else:
                        w = [M.act(e, BC[:, 0, t0:512 * hf + 512], ACT.Exp, bias=g, after=[*bw, *rows, *prior])]
                    pr = M.tt(PP[:, i % 2, o:512], sc, e, MUL, after=[t, *w, *use.get(("pp", i % 2), [])])
                    use[("p", i % 2)] = [pr]
                    Q.give(bk, [pr])
                    return o, pr
                nxt = score(0)
                for i in items:
                    o, pr = nxt
                    if i + 1 < len(items):
                        nxt = score(i + 1)
                    M.mm(Q.t[:, acc[0], o:512], VT[:, b, i, s * 128:(s + 1) * 128], PP[:, i % 2, o:512], i == 0, i == items[-1],
                         after=[pr, *afree, *inw[j]])
                    t = M.mm(Q.t[:, acc[1], o:512], C.ones[:, :], PP[:, i % 2, o:512], i == 0, i == items[-1], inc=True)
                    use[("pp", i % 2)] = [t]
                    yield
                sl = slice(hf * 512, hf * 512 + 512)
                a = M.act(dd[:, :], Q.t[:, acc[1], :], ACT.Abs, after=[t, *use.get("dd", [])])
                Q.give([acc[1]], [a])
                u = M.tt(dd[:, :], dd[:, :], BC[:, 1, sl], MAX, after=[a, *bw])
                u = M.recip(dd[:, :], dd[:, :], after=[u])
                u = M.tt(hh[:, :], Q.t[:, acc[0], :], dd[:, :], MUL, after=[u, *use.get("hh", [])])
                Q.give([acc[0]], [u])
                a = M.act(dd[:, :], hh[:, :], ACT.Square, after=[u])
                bk, free = Q.take(1)
                t = M.mm(Q.t[:, bk[0], :], C.ones[:, :], dd[:, :], True, True, after=[*free, a], inc=True)
                a = M.act(dd[:, :], Q.t[:, bk[0], :], ACT.Sqrt, after=[t], bias=C.eps[:, 0:1], scale=1.0 / 128)
                Q.give(bk, [a])
                u = M.recip(dd[:, :], dd[:, :], after=[a])
                u = M.stt(Y[:, h, sl], hh[:, :], pv("ml_head_g", h), dd[:, :], MUL, MUL, after=[u])
                use["dd"] = use["hh"] = [u]
                use["bc"] = [u]
                yw[h] = [u]
                yield
        use[b] = [M.T.now()]

    def gates():
        def evac(m, ps, tok):
            t = M.act(ps, ps, ACT.Sigmoid, after=[tok], bias=pv("ml_b_in", 16 + m))
            u = M.tt(Y[:, m, :], Y[:, m, :], ps, MUL, after=[t, *yw[m]])
            yw[m] = [u]
            return [u]
        yield from dense(M, W, P, hk, 8, evac)

    run(project(0))
    for j in range(3):
        side_by_side(heads(j), 30, project(j + 1), 32)
    side_by_side(heads(3), 30, gates(), 44)
    M.fence()
    c1.close()
    c2.close()
    g = mix_out(M, W, P, C, X, {i: Y[:, i, :] for i in range(8)}, yw, lambda i: pv("post_mix_g1", i))
    next(g)
    c.close()
    run(g)


VECTORS = ["pre_mix_g0", "pre_mix_g1", "post_mix_g0", "post_mix_g1", "pre_ffn_g0", "pre_ffn_g1", "post_ffn_g0", "post_ffn_g1",
           "ab_b_in", "conf_conv_b", "conf_ln_g", "conf_ln_b", "lru_conv_b", "lru_b_a", "lru_b_x", "lru_lambda", "ml_head_g"]



NEG = -1e30
SLOPES = [2.0 ** (-8.0 * (h + 1) / 4) for h in range(4)]


class Filler:

    def __init__(self, gen):
        self.gen, self.inside = gen, False

    def step(self):
        got = next(self.gen, 0)
        self.inside = got is None

    def align(self):
        while self.inside:
            self.step()

    def blend(self, gen, rate):
        due = 0.0
        self.align()
        for _ in gen:
            due += rate
            while due >= 1:
                due -= 1
                self.step()


def transpose_tiles(M, Q, C, src, dst, after, reuse=()):
    out = []
    for q in range(2):
        bk, free = Q.take(1)
        for i in range(4):
            t = M.tr(Q.t[:, bk[0], i * 128:(i + 1) * 128], src[:, (4 * q + i) * 128:(4 * q + i + 1) * 128], C.ident,
                     after=[*after, *free], inc=(i == 3))
        u = M.cp(dst[:, 4 * q:4 * q + 4, :], Q.t[:, bk[0], :].rearrange("p (a b) -> p a b", a=4), after=[t, *reuse])
        Q.give(bk, [u])
        out = [u, t]
        yield
    return out


def by_ones(M, Q, C, ones, src, after, use):
    out = []
    for h in range(2):
        bk, free = Q.take(1)
        sl = slice(h * 512, h * 512 + 512)
        t = M.mm(Q.t[:, bk[0], :], ones, src[:, sl], True, True, after=[*after, *free], inc=True)
        u = use(sl, Q.t[:, bk[0], :], [t])
        Q.give(bk, [u])
        out.append(u)
    return out


def head_rstd(M, Q, C, src, sq, out, after, eps, width=64):
    a = M.act(sq, src, ACT.Square, after=after)
    w = by_ones(M, Q, C, C.heads, sq, [a], lambda sl, ps, t: M.act(out[:, sl], ps, ACT.Sqrt, after=t, bias=eps, scale=1.0 / width))
    return M.recip(out, out, after=w)


class Inverse:

    def __init__(self, M, ctx):
        self.AT, self.T, self.TT, self.X = (M.sb([128, 512], ctx=ctx, name="inv") for _ in range(4))
        self.idle = []

    def steps(self, M, Q, C, after):
        four = lambda x: x.unsqueeze(1).to_broadcast([128, 4, 128])
        v4 = lambda x: x.rearrange("p (a b) -> p a b", a=4)
        t = M.tt(v4(self.TT[:, :]), v4(self.AT[:, :]), four(C.level[0]), MUL, after=[*after, *self.idle])
        tt = M.tt(v4(self.TT[:, :]), four(C.ident), v4(self.TT[:, :]), SUB, after=[t])
        bk, free = Q.take(1)
        for i in range(4):
            s = slice(i * 128, i * 128 + 128)
            p = M.tr(Q.t[:, bk[0], s], self.TT[:, s], C.ident, after=[tt, *free], inc=(i == 3))
        tn = M.act(self.T[:, :], Q.t[:, bk[0], :], ACT.Copy, after=[p])
        Q.give(bk, [tn])
        yield
        for b in range(1, 7):
            m = M.tt(v4(self.X[:, :]), v4(self.AT[:, :]), four(C.level[b]), MUL, after=[tt], eng=M.G)
            bk, free = Q.take(1)
            for i in range(4):
                s = slice(i * 128, i * 128 + 128)
                p = M.mm(Q.t[:, bk[0], s], self.X[:, s], self.T[:, s], True, True, after=[m, tn, *free], inc=(i == 3))
            x = M.act(self.X[:, :], Q.t[:, bk[0], :], ACT.Copy, after=[p])
            Q.give(bk, [x])
            yield
            bk, free = Q.take(1)
            for i in range(4):
                s = slice(i * 128, i * 128 + 128)
                p = M.mm(Q.t[:, bk[0], s], self.X[:, s], self.TT[:, s], True, True, after=[x, tt, *free], inc=(i == 3))
            if b < 6:
                b2, f2 = Q.take(1)
                for i in range(4):
                    s = slice(i * 128, i * 128 + 128)
                    p2 = M.mm(Q.t[:, b2[0], s], self.TT[:, s], self.X[:, s], True, True, after=[x, *f2], inc=(i == 3))
                tn = M.tt(self.T[:, :], self.T[:, :], Q.t[:, b2[0], :], SUB, after=[p2])
                Q.give(b2, [tn])
                tt = M.tt(self.TT[:, :], self.TT[:, :], Q.t[:, bk[0], :], SUB, after=[p, p2])
            else:
                tt = M.tt(self.TT[:, :], self.TT[:, :], Q.t[:, bk[0], :], SUB, after=[p])
            Q.give(bk, [tt])
            yield
        self.done = [tt]


def both(a, b):
    live = [a, b]
    while live:
        for g in list(live):
            if next(g, StopIteration) is StopIteration:
                live.remove(g)
        yield


def pair_products(M, Q, p0, lhs, rhs, q, after, use):
    bk, free = Q.take(1)
    for i in range(4):
        n = slice((4 * q + i) * 128, (4 * q + i) * 128 + 128)
        t = M.mm(Q.t[:, bk[0], i * 128:i * 128 + 128], lhs[p0:p0 + 64, n], rhs[p0:p0 + 64, n], True, True, after=[*after, *free], inc=(i == 3))
    u = use(Q.t[:, bk[0], :], [t])
    Q.give(bk, [u])
    return [u]


def gdn(M, W, P, Q, C, hk, j, ZY, small, vec):
    s0 = Scope()
    sb = lambda *sh: M.sb([128, *sh], ctx=s0, name="g")
    EG, QI = sb(T), sb(T)
    VB, KG, KO = sb(8, 128), sb(8, 128), sb(8, 128)
    O, S = sb(T), sb(128)
    sQ = Scope()
    Qn, Kn, KB, V = (M.sb([128, T], ctx=sQ) for _ in range(4))
    s1 = Scope()
    raw = M.sb([128, 3, 3 + T], ctx=s1)
    z = M.fill(raw[:, :, 0:3], 0.0, eng=M.G)
    w = {}

    def evac(m, ps, tok):
        if m < 3:
            w[m] = [M.act(raw[:, m, 3:], ps, ACT.Copy, after=[tok]), z]
        else:
            w[m] = [M.act(ZY, ps, ACT.Silu, after=[tok])]
        return w[m][:1]
    run(dense(M, W, P, hk, 4, evac))
    sq, rs = M.sb([128, T], ctx=s1), M.sb([128, T], ctx=s1)
    for m, dst in enumerate((Qn, Kn, V)):
        t = conv(M, dst[:, :], raw[:, m, :], vec(f"gdn_conv{2 * m + j}", 0, 4), None, 4, w[m])
        a = M.act(dst[:, :], dst[:, :], ACT.Silu, after=[t])
        w[m] = [a]
        yield
    for m, dst in enumerate((Qn, Kn)):
        r = head_rstd(M, Q, C, dst[:, :], sq[:, :], rs[:, :], [*w[m], *(w[0] if m else [])], C.eps[:, 0:1], 1)
        w[m] = [M.stt(dst[:, :], dst[:, :], 0.125 if m == 0 else 1.0, rs[:, :], MUL, MUL, after=[r])]
        yield
    s1.close()
    M.fence()
    s1 = Scope()
    BB, GB, EL, tmp = (M.sb([128, T], ctx=s1) for _ in range(4))
    bw = by_ones(M, Q, C, C.pair[32:36, j, :], small.rows[32:36, :], small.w, lambda sl, ps, t: M.act(BB[:, sl], ps, ACT.Copy, after=t))
    gw = by_ones(M, Q, C, C.pair[0:4, j, :], small.rows[0:4, :], small.w, lambda sl, ps, t: M.cp(GB[:, sl], ps, after=t))
    yield
    t3 = lambda x: x.rearrange("p (a b) -> p a b", a=8)
    eg = M.act(EG[:, :], GB[:, :], ACT.Exp, after=gw)
    last = t3(GB[:, :])[:, :, 127:128].to_broadcast([128, 8, 128])
    u = M.tt(t3(EL[:, :]), last, t3(GB[:, :]), SUB, after=gw)
    el = M.act(EL[:, :], EL[:, :], ACT.Exp, after=[u])
    qi = M.tt(QI[:, :], Qn[:, :], EG[:, :], MUL, after=[eg, *w[0]], eng=M.G)
    kb = M.tt(KB[:, :], Kn[:, :], BB[:, :], MUL, after=[*bw, *w[1]])
    u = M.tt(V[:, :], V[:, :], BB[:, :], MUL, after=[*bw, *w[2]])
    vt = yield from transpose_tiles(M, Q, C, V[:, :], VB, [u])
    u = M.tt(tmp[:, :], KB[:, :], EG[:, :], MUL, after=[kb, eg])
    kg = yield from transpose_tiles(M, Q, C, tmp[:, :], KG, [u])
    u = M.tt(EL[:, :], Kn[:, :], EL[:, :], MUL, after=[el])
    ko = yield from transpose_tiles(M, Q, C, EL[:, :], KO, [u])
    s1.close()
    M.fence()
    s1 = Scope()
    inv = [Inverse(M, s1) for _ in range(2)]
    ATT = M.sb([128, 2, 4, 128], ctx=s1)
    U, WT = M.sb([128, 4, 128], ctx=s1), M.sb([128, 512], ctx=s1)
    DT = M.sb([128, 2, 512], ctx=s1)
    VN = M.sb([128, 2, 128], ctx=s1)
    sw = [M.fill(S[:, :], 0.0)]
    ow = []
    used = []
    for q in range(2):
        hold = {}

        def head(s):
            h, p0 = 2 * j + s, 64 * s
            D = DT[:, s, :].rearrange("p (a b) -> p a b", a=4)
            bk, free = Q.take(1)
            t = M.mm(Q.t[:, bk[0], :], C.sel[0:4, h, :], small.rows[0:4, q * 512:q * 512 + 512], True, True, after=[*free, *small.w], inc=True)
            g = small.gT[:, 4 * q:4 * q + 4, h:h + 1].to_broadcast([128, 4, 128])
            u = M.tt(D, Q.t[:, bk[0], :].rearrange("p (a b) -> p a b", a=4), g, SUB, after=[t, *used])
            Q.give(bk, [u])
            u = M.ts(DT[:, s, :], DT[:, s, :], 0.0, MIN, after=[u])
            a = M.act(DT[:, s, :], DT[:, s, :], ACT.Exp, after=[u])
            dw = M.tt(D, D, C.upper.unsqueeze(1).to_broadcast([128, 4, 128]), MUL, after=[a])
            yield
            aw = pair_products(M, Q, p0, Kn, KB, q, [kb, *w[1]], lambda ps, t: M.tt(inv[s].AT[:, :], ps, DT[:, s, :], MUL, after=[*t, dw, *used]))
            tw = pair_products(M, Q, p0, Kn, Qn, q, [*w[0]], lambda ps, t: M.tt(ATT[:, s, :, :].rearrange("p a b -> p (a b)"), ps, DT[:, s, :], MUL, after=[*t, dw, *used]))
            yield
            yield from inv[s].steps(M, Q, C, aw)
            bk, free = Q.take(1)
            for i in range(4):
                t = M.mm(Q.t[:, bk[0], i * 64:i * 64 + 64], inv[s].TT[:, i * 128:i * 128 + 128], VB[:, 4 * q + i, p0:p0 + 64], True, True,
                         after=[*free, *inv[s].done, vt[0]], inc=(i == 3))
            u = M.cp(U[:, :, p0:p0 + 64], Q.t[:, bk[0], 0:256].rearrange("p (a b) -> p a b", a=4), after=[t, *used])
            Q.give(bk, [u])
            bk, free = Q.take(1)
            for i in range(4):
                t = M.mm(Q.t[p0:p0 + 64, bk[0], i * 128:i * 128 + 128], KG[:, 4 * q + i, p0:p0 + 64], inv[s].TT[:, i * 128:i * 128 + 128], True, True,
                         after=[*free, kg[0]], inc=(i == 3))
            x = M.act(WT[p0:p0 + 64, :], Q.t[p0:p0 + 64, bk[0], :], ACT.Copy, after=[t, *used])
            Q.give(bk, [x])
            inv[s].idle = [t]
            hold[s] = [u, x, *tw]
            yield
        yield from both(head(0), head(1))
        for i in range(4):
            n = 4 * q + i
            sl = slice(n * 128, n * 128 + 128)
            bk, free = Q.take(1)
            t = M.mm(Q.t[:, bk[0], 0:128], WT[:, i * 128:i * 128 + 128], S[:, :], True, True, after=[*free, *hold[0], *hold[1], *sw], inc=True)
            vn = M.tt(VN[:, i % 2, :], U[:, i, :], Q.t[:, bk[0], 0:128], SUB, after=[t])
            Q.give(bk, [vn])
            bo, fo = Q.take(1)
            M.mm(Q.t[:, bo[0], 0:128], S[:, :], QI[:, sl], True, False, after=[*fo, qi])
            for s in range(2):
                t = M.mm(Q.t[64 * s:64 * s + 64, bo[0], 0:128], VN[:, i % 2, 64 * s:64 * s + 64], ATT[:, s, i, :], False, True,
                         after=[vn], inc=(s == 1))
            a = M.act(O[:, sl], Q.t[:, bo[0], 0:128], ACT.Copy, after=[t])
            Q.give(bo, [a])
            ow = [a]
            bs, fs = Q.take(1)
            ts_ = M.mm(Q.t[:, bs[0], 0:128], KO[:, n, :], VN[:, i % 2, :], True, True, after=[*fs, ko[0]], inc=True)
            sw = []
            for s in range(2):
                p = slice(64 * s, 64 * s + 64)
                sw = [M.stt(S[p, p], S[p, p], EG[p, n * 128 + 127:n * 128 + 128], Q.t[p, bs[0], p], MUL, ADD, after=[ts_, eg])]
            Q.give(bs, sw)
            yield
        used = [M.T.now(), *sw]
    s1.close()
    sQ.close()
    M.fence()
    s1 = Scope()
    sq, rs = M.sb([128, T], ctx=s1), M.sb([128, T], ctx=s1)
    r = head_rstd(M, Q, C, O[:, :], sq[:, :], rs[:, :], ow, C.eps[:, 0:1])
    yield
    u = M.stt(O[:, :], O[:, :], vec("gdn_norm", 0), rs[:, :], MUL, MUL, after=[r])
    u = M.tt(ZY, O[:, :], ZY, MUL, after=[u, *w[3]])
    small.y = [u]
    s1.close()
    s0.close()
    M.fence()


def head_layernorm(M, Q, C, x, sq, rs, after, eps, gain, bias):
    w = by_ones(M, Q, C, C.heads, x, after, lambda sl, ps, t: M.stt(sq[:, sl], ps, -1.0 / 64, x[:, sl], MUL, ADD, after=t))
    u = M.cp(x, sq, after=w)
    r = head_rstd(M, Q, C, x, sq, rs, [u], eps)
    u = M.tt(x, x, rs, MUL, after=[r])
    return M.ts(x, x, gain, MUL, bias, ADD, after=[u])


def spatial(M, W, P, Q, C, hk, j, ZY, small, vec):
    s0 = Scope()
    U, V, sq, rs = (M.sb([128, T], ctx=s0) for _ in range(4))
    VT = M.sb([128, 8, 128], ctx=s0)
    w = {}

    def evac(m, ps, tok):
        dst, f = ((U[:, :], ACT.Gelu_apprx_tanh), (V[:, :], ACT.Gelu_apprx_tanh), (ZY, ACT.Silu))[m]
        w[m] = [M.act(dst, ps, f, after=[tok])]
        return w[m]
    run(dense(M, W, P, hk, 3, evac))
    u = head_layernorm(M, Q, C, V[:, :], sq[:, :], rs[:, :], w[1], C.eps5[:, 0:1], vec("sg_ln_gain", j), vec("sg_ln_bias", j))
    yield
    t = yield from transpose_tiles(M, Q, C, V[:, :], VT, [u])
    uz = M.tt(U[:, :], U[:, :], ZY, MUL, after=[*w[0], *w[2]])
    for q in range(2):
        bk, free = Q.take(1)
        for i in range(4):
            n = 4 * q + i
            o = slice(i * 128, i * 128 + 128)
            M.mm(Q.t[:, bk[0], o], C.pair[0:4, j, :], C.sg_b[0:4, :], True, False, after=free)
            for s in range(2):
                m = M.mm(Q.t[64 * s:64 * s + 64, bk[0], o], VT[:, n, 64 * s:64 * s + 64], C.sg_w[:, 2 * j + s, :], False, True,
                         after=[t[0]], inc=(i == 3 and s == 1))
        sl = slice(q * 512, q * 512 + 512)
        u = M.tt(ZY[:, sl], U[:, sl], Q.t[:, bk[0], :], MUL, after=[m, uz])
        Q.give(bk, [u])
        yield
    small.y = [u]
    s0.close()
    M.fence()


def rwkv(M, W, P, Q, C, hk, j, ZY, small, vec, WA, waw):
    s0 = Scope()
    sb = lambda *sh: M.sb([128, *sh], ctx=s0, name="r")
    R0, BON, O, S = sb(T), sb(T), sb(T), sb(128)
    Vt, A0, K1, B1 = sb(8, 128), sb(8, 128), sb(8, 128), sb(8, 128)
    CM, CC, ECM, ECC, EC = sb(8), sb(8), sb(8), sb(8), sb(8)
    omk = sb(1)
    sF = Scope()
    AL, BE, KA, RO = (M.sb([128, T], ctx=sF) for _ in range(4))
    s1 = Scope()
    pad = M.sb([128, 1 + T], ctx=s1)
    V, Cs, Aa, tmp = (M.sb([128, T], ctx=s1) for _ in range(4))
    z = M.fill(pad[:, 0:1], 0.0)
    w = {}
    dst = [KA, RO, V]
    mu = [2 + j, j, 4 + j]
    hold = {"f": [z]}

    def evac(m, ps, tok):
        if m == 3:
            w[3] = [M.act(ZY, ps, ACT.Silu, after=[tok])]
            return w[3]
        a = M.act(pad[:, 1:], ps, ACT.Copy, after=[tok, *hold["f"]])
        u = M.tt(tmp[:, :], pad[:, 0:T], pad[:, 1:], SUB, after=[a])
        u = M.stt(dst[m][:, :], tmp[:, :], vec("rw_mu", mu[m]), pad[:, 1:], MUL, ADD, after=[u])
        hold["f"] = w[m] = [u]
        return [a]
    run(dense(M, W, P, hk, 4, evac))
    cols = slice(j * 128, j * 128 + 128)
    lw = by_ones(M, Q, C, C.rw_up[0:64, cols], WA[0:64, :], waw, lambda sl, ps, t: M.act(tmp[:, sl], ps, ACT.Sigmoid, after=[*t, *w[2]], bias=vec("rw_w0", j)))
    aw = by_ones(M, Q, C, C.rw_up[64:128, cols], WA[64:128, :], waw, lambda sl, ps, t: M.act(Aa[:, sl], ps, ACT.Sigmoid, after=t, bias=vec("rw_a0", j)))
    yield
    u = M.ts(tmp[:, :], tmp[:, :], -float(np.exp(-0.5)), MUL, after=lw)
    zz = M.fill(AL[:, :], 0.0)
    for n in range(8):
        sl = slice(n * 128, n * 128 + 128)
        u = M.scan(Cs[:, sl], tmp[:, sl], AL[:, sl], 0.0, ADD, ADD, after=[u, zz])
        yield
    t3 = lambda x: x.rearrange("p (a b) -> p a b", a=8)
    wide = lambda x: x.unsqueeze(2).to_broadcast([128, 8, 128])
    u = M.cp(CM[:, :], t3(Cs[:, :])[:, :, 63], after=[u])
    u = M.cp(CC[:, :], t3(Cs[:, :])[:, :, 127], after=[u])
    e0 = M.act(ECM[:, :], CM[:, :], ACT.Exp, after=[u])
    e1 = M.act(EC[:, :], CC[:, :], ACT.Exp, after=[u])
    u = M.tt(CC[:, :], CC[:, :], CM[:, :], SUB, after=[e1])
    e2 = M.act(ECC[:, :], CC[:, :], ACT.Exp, after=[u])
    u = M.tt(t3(Cs[:, :]), t3(Cs[:, :]), wide(CM[:, :]), SUB, after=[u])
    k = M.ts(AL[:, :], KA[:, :], vec("rw_k_k", j), MUL, after=w[0])
    r = head_rstd(M, Q, C, AL[:, :], pad[:, 0:T], BE[:, :], [k, *w[2]], C.eps[:, 0:1], 1)
    k = M.tt(AL[:, :], AL[:, :], BE[:, :], MUL, after=[r])
    yield
    b = M.tt(BE[:, :], AL[:, :], Aa[:, :], MUL, after=[k, *aw])
    x = M.ts(omk[:, :], vec("rw_k_a", j), -1.0, MUL, 1.0, ADD)
    x = M.ts(Aa[:, :], Aa[:, :], vec("rw_k_a", j), MUL, omk[:, 0:1], ADD, after=[x, b])
    kp = M.tt(KA[:, :], KA[:, :], Aa[:, :], MUL, after=[x])
    x = M.stt(Aa[:, :], KA[:, :], vec("rw_r_k", j), RO[:, :], MUL, MUL, after=[kp, *w[1]])
    bonus = by_ones(M, Q, C, C.heads, Aa, [x], lambda sl, ps, t: M.tt(BON[:, sl], ps, V[:, sl], MUL, after=[*t, *w[2]]))
    yield
    vt = yield from transpose_tiles(M, Q, C, V[:, :], Vt, w[2])
    x = M.tt(tmp[:, :], Cs[:, :], tmp[:, :], SUB, after=[u])
    e = M.act(tmp[:, :], tmp[:, :], ACT.Exp, after=[x])
    al = M.tt(AL[:, :], AL[:, :], tmp[:, :], MUL, after=[e])
    e = M.act(tmp[:, :], Cs[:, :], ACT.Exp, after=[al])
    ro = M.tt(RO[:, :], RO[:, :], tmp[:, :], MUL, after=[e])
    e = M.act(tmp[:, :], Cs[:, :], ACT.Exp, after=[ro], scale=-1.0)
    be = M.tt(BE[:, :], BE[:, :], tmp[:, :], MUL, after=[e])
    ka = M.tt(KA[:, :], KA[:, :], tmp[:, :], MUL, after=[e])
    r0 = M.tt(t3(R0[:, :]), t3(RO[:, :]), wide(ECM[:, :]), MUL, after=[ro, e0])
    yield
    x = M.tt(t3(V[:, :]), t3(AL[:, :]), wide(ECM[:, :]), MUL, after=[al, vt[1], *bonus])
    a0 = yield from transpose_tiles(M, Q, C, V[:, :], A0, [x])
    x = M.tt(t3(Cs[:, :]), t3(KA[:, :]), wide(ECC[:, :]), MUL, after=[ka, e2])
    k1 = yield from transpose_tiles(M, Q, C, Cs[:, :], K1, [x])
    x = M.tt(t3(Aa[:, :]), t3(BE[:, :]), wide(ECC[:, :]), MUL, after=[be, M.T.now()])
    b1 = yield from transpose_tiles(M, Q, C, Aa[:, :], B1, [x])
    s1.close()
    M.fence()
    s1 = Scope()
    inv = [Inverse(M, s1) for _ in range(2)]
    CK, CB = M.sb([128, 2, 512], ctx=s1), M.sb([128, 2, 512], ctx=s1)
    U, WT = M.sb([128, 4, 128], ctx=s1), M.sb([128, 512], ctx=s1)
    VN = M.sb([128, 2, 128], ctx=s1)
    BVt = O[:, 512:].rearrange("p (a b c) -> p a b c", a=2, b=4)
    sw = [M.fill(S[:, :], 0.0)]
    ow, used = [], []
    four = lambda x: x.unsqueeze(1).to_broadcast([128, 4, 128])
    v4 = lambda x: x.rearrange("p (a b) -> p a b", a=4)
    for q in range(2):
        hold = {}

        def head(s):
            p0 = 64 * s
            iv = inv[s]
            aw = pair_products(M, Q, p0, BE, AL, q, [be, al], lambda ps, t: M.tt(v4(iv.AT[:, :]), v4(ps), four(C.upper), MUL, after=[*t, *used]))
            bw = pair_products(M, Q, p0, KA, AL, q, [ka], lambda ps, t: M.tt(v4(iv.X[:, :]), v4(ps), four(C.strict), MUL, after=[*t, *used]))
            yield
            kw = pair_products(M, Q, p0, KA, RO, q, [ro], lambda ps, t: M.tt(v4(CK[:, s, :]), v4(ps), four(C.upper), MUL, after=[*t, *used]))
            rw = pair_products(M, Q, p0, BE, RO, q, [ro], lambda ps, t: M.tt(v4(CB[:, s, :]), v4(ps), four(C.upper), MUL, after=[*t, *used]))
            yield
            bk, free = Q.take(1)
            for i in range(4):
                t = M.mm(Q.t[:, bk[0], i * 64:i * 64 + 64], iv.X[:, i * 128:i * 128 + 128], Vt[:, 4 * q + i, p0:p0 + 64], True, True,
                         after=[*free, *bw, vt[0]], inc=(i == 3))
            bv = M.cp(BVt[:, s, :, :], Q.t[:, bk[0], 0:256].rearrange("p (a b) -> p a b", a=4), after=[t, *used])
            Q.give(bk, [bv])
            yield
            yield from iv.steps(M, Q, C, [*aw, bv])
            bk, free = Q.take(1)
            for i in range(4):
                t = M.mm(Q.t[:, bk[0], i * 64:i * 64 + 64], iv.TT[:, i * 128:i * 128 + 128], BVt[:, s, i, :], True, True,
                         after=[*free, *iv.done, bv], inc=(i == 3))
            u = M.cp(U[:, :, p0:p0 + 64], Q.t[:, bk[0], 0:256].rearrange("p (a b) -> p a b", a=4), after=[t, *used])
            Q.give(bk, [u])
            bk, free = Q.take(1)
            for i in range(4):
                t = M.mm(Q.t[p0:p0 + 64, bk[0], i * 128:i * 128 + 128], A0[:, 4 * q + i, p0:p0 + 64], iv.TT[:, i * 128:i * 128 + 128], True, True,
                         after=[*free, a0[0]], inc=(i == 3))
            x = M.act(WT[p0:p0 + 64, :], Q.t[p0:p0 + 64, bk[0], :], ACT.Copy, after=[t, *used])
            Q.give(bk, [x])
            iv.idle = [t]
            hold[s] = [u, x, *kw, *rw]
            yield
        yield from both(head(0), head(1))
        for i in range(4):
            n = 4 * q + i
            sl = slice(n * 128, n * 128 + 128)
            bk, free = Q.take(1)
            t = M.mm(Q.t[:, bk[0], 0:128], WT[:, i * 128:i * 128 + 128], S[:, :], True, True, after=[*free, *hold[0], *hold[1], *sw], inc=True)
            vn = M.stt(VN[:, i % 2, :], Q.t[:, bk[0], 0:128], -1.0, U[:, i, :], MUL, SUB, after=[t])
            Q.give(bk, [vn])
            bo, fo = Q.take(1)
            M.mm(Q.t[:, bo[0], 0:128], S[:, :], R0[:, sl], True, False, after=[*fo, r0])
            for s in range(2):
                o = Q.t[64 * s:64 * s + 64, bo[0], 0:128]
                M.mm(o, Vt[:, n, 64 * s:64 * s + 64], CK[:, s, i * 128:i * 128 + 128], False, False)
                t = M.mm(o, VN[:, i % 2, 64 * s:64 * s + 64], CB[:, s, i * 128:i * 128 + 128], False, True, after=[vn], inc=(s == 1))
            a = M.act(O[:, sl], Q.t[:, bo[0], 0:128], ACT.Copy, after=[t])
            Q.give(bo, [a])
            ow = [a]
            bs, fs = Q.take(1)
            M.mm(Q.t[:, bs[0], 0:128], K1[:, n, :], Vt[:, n, :], True, False, after=[*fs, k1[0]])
            ts_ = M.mm(Q.t[:, bs[0], 0:128], B1[:, n, :], VN[:, i % 2, :], False, True, after=[b1[0]], inc=True)
            for s in range(2):
                p = slice(64 * s, 64 * s + 64)
                sw = [M.stt(S[p, p], S[p, p], EC[p, n:n + 1], Q.t[p, bs[0], p], MUL, ADD, after=[ts_])]
            Q.give(bs, sw)
            yield
        used = [M.T.now(), *sw]
    s1.close()
    sF.close()
    M.fence()
    s1 = Scope()
    sq, rs = M.sb([128, T], ctx=s1), M.sb([128, T], ctx=s1)
    u = head_layernorm(M, Q, C, O[:, :], sq[:, :], rs[:, :], ow, C.epsgn[:, 0:1], vec("rw_gn_gain", j), vec("rw_gn_bias", j))
    yield
    u = M.tt(O[:, :], O[:, :], BON[:, :], ADD, after=[u])
    u = M.tt(ZY, O[:, :], ZY, MUL, after=[u, *w[3]])
    small.y = [u]
    s1.close()
    s0.close()
    M.fence()


def nsa(M, W, P, Q, C, A, hk, small, vec, done, sem_of, fill):
    s0 = Scope()
    QF = M.sb([128, 2, T], ctx=s0)
    KS, KW = M.sb([128, T], ctx=s0), M.sb([128, T], ctx=s0)
    VSW = M.sb([128, 8, 128], ctx=s0)
    Y = M.sb([128, 8, 256], ctx=s0)
    SELN = M.sb([128, 8, 16], ctx=s0)
    s1 = Scope()
    KVC, VF = M.sb([128, T], ctx=s1), M.sb([128, T], ctx=s1)
    w = {}
    dst = [KVC[:, :], KS[:, :], KW[:, :], VF[:, :], QF[:, 0, :], QF[:, 1, :]]

    def evac(m, ps, tok):
        w[m] = [M.act(dst[m], ps, ACT.Copy, after=[tok])]
        return w[m]
    run(dense(M, W, P, hk, 6, evac))
    vsw = yield from transpose_tiles(M, Q, C, VF[:, :], VSW, w[3])
    W1 = M.sb([128, 32, 64], ctx=s1)
    POS = M.sb([128, 32], ctx=s1)
    W2 = M.sb([128, 128], ctx=s1)
    CB = M.sb([128, 8, 4, 64], ctx=s1)
    CM = M.sb([128, 8, 64], ctx=s1)
    FR = M.sb([128, 8, 16], ctx=s1)
    INT = M.sb([128, 16], ctx=s1)
    ld, loads = sem_of(), []
    pairs = ((W1[:, :, :], A["cmp_w1"]), (POS[:, :], A["cmp_pos"]), (W2[:, :], A["cmp_w2"]), (CB[:, :, :, :], A["c_bias"]),
             (CM[:, :, :], A["c_mask"]), (FR[:, :, :], A["c_force"]), (INT[:, :], A["c_inter"]))
    start = M.fence()
    for d, s in pairs:
        loads = [M.Y.load(lambda e, d=d, s=s: e.dma_start(d, s), ld, 16 * len(pairs), after=start)]
    HK = M.sb([128, 64], ctx=s1)
    PB = M.sb([128, 2], ctx=s1)
    KC, VC = M.sb([128, 64], ctx=s1), M.sb([128, 64], ctx=s1)
    PC = M.sb([128, 8, 4, 64], ctx=s1)
    PT = M.sb([128, 2, T], ctx=s1)
    mx = M.sb([128, 32], ctx=s1)
    z = M.fill(HK[:, :], 0.0)
    hw = []
    for r in range(2):
        p = slice(64 * r, 64 * r + 64)
        bk, free = Q.take(1)
        for l in range(32):
            M.mm(Q.t[p, bk[0], 0:63], W1[p, l, :], KVC[p, l:l + 993:16], l == 0, l == 31, after=[*free, *loads, *w[0]])
        for l in range(32):
            t = M.mm(Q.t[p, bk[0], 64:66], W1[p, l, :], POS[p, l:l + 1].to_broadcast([64, 2]), l == 0, l == 31, inc=(l == 31))
        a = M.act(PB[p, :], Q.t[p, bk[0], 64:66], ACT.Copy, after=[t])
        a = M.act(HK[p, 0:63], Q.t[p, bk[0], 0:63], ACT.Gelu_apprx_tanh, after=[a, z], bias=PB[p, 0:1])
        Q.give(bk, [a])
        hw.append(a)
        yield
    bk, free = Q.take(1)
    t = M.mm(Q.t[:, bk[0], 0:64], W2[0:64, :], HK[0:64, :], True, True, after=[*free, *hw], inc=True)
    kc = M.cp(KC[:, :], Q.t[:, bk[0], 0:64], after=[t])
    Q.give(bk, [kc])
    bk, free = Q.take(1)
    for r in range(2):
        t = M.mm(Q.t[64 * r:64 * r + 64, bk[0], 0:64], HK[64:128, :], W2[64:128, 0:64], True, True, after=[*free, *hw], inc=(r == 1))
    vc = M.cp(VC[:, :], Q.t[:, bk[0], 0:64], after=[t])
    Q.give(bk, [vc])
    for h in range(4):
        p = slice(64 * (h % 2), 64 * (h % 2) + 64)
        bk, free = Q.take(1)
        for n in range(8):
            t = M.mm(Q.t[:, bk[0], n * 64:n * 64 + 64], QF[p, h // 2, n * 128:n * 128 + 128], KC[p, :], True, True,
                     after=[*free, kc, *w[4], *w[5]], inc=(n == 7))
        u = M.stt(PC[:, :, h, :], Q.t[:, bk[0], :].rearrange("p (a b) -> p a b", a=8), 0.125, CB[:, :, h, :], MUL, ADD, after=[t, *loads])
        Q.give(bk, [u])
        yield
    flat = PC[:, :, :, :].rearrange("p a b c -> p (a b) c")
    red = lambda out, src, op, after: M.V.put(lambda e: e.tensor_reduce(out, src, AX, op), after)
    over = lambda x: x.unsqueeze(2).to_broadcast([128, 32, 64])
    u = red(mx[:, :], flat, MAX, [u])
    u = M.tt(flat, flat, over(mx[:, :]), SUB, after=[u])
    a = M.act(flat, flat, ACT.Exp, after=[u])
    u = red(mx[:, :], flat, ADD, [a])
    u = M.recip(mx[:, :], mx[:, :], after=[u])
    for h in range(4):
        u = M.tt(PC[:, :, h, :], PC[:, :, h, :], CM[:, :, :], MUL, after=[u])
    u = M.tt(flat, flat, over(mx[:, :]), MUL, after=[u])
    yield
    pt = []
    for pr in range(2):
        for q in range(2):
            bk, free = Q.take(1)
            for i in range(4):
                t = M.tr(Q.t[:, bk[0], i * 128:i * 128 + 128], PC[:, 4 * q + i, 2 * pr:2 * pr + 2, :].rearrange("p a b -> p (a b)"), C.ident,
                         after=[*free, u], inc=(i == 3))
            pt = [M.cp(PT[:, pr, q * 512:q * 512 + 512], Q.t[:, bk[0], :], after=[t])]
            Q.give(bk, pt)
            yield
    yw = []
    for h in range(4):
        p = slice(64 * (h % 2), 64 * (h % 2) + 64)
        bk, free = Q.take(1)
        for n in range(8):
            t = M.mm(Q.t[:, bk[0], n * 64:n * 64 + 64], PT[p, h // 2, n * 128:n * 128 + 128], VC[p, :], True, True,
                     after=[*free, *pt, vc], inc=(n == 7))
        yw = [M.tt(Y[:, :, h * 64:h * 64 + 64], Q.t[:, bk[0], :].rearrange("p (a b) -> p a b", a=8),
                   small.gate[:, :, 3 * h:3 * h + 1].to_broadcast([128, 8, 64]), MUL, after=[t, *small.w])]
        Q.give(bk, yw)
        yield
    bk, free = Q.take(1)
    for n in range(8):
        for pr in range(2):
            t = M.mm(Q.t[:, bk[0], n * 16:n * 16 + 16], PT[:, pr, n * 128:n * 128 + 128], INT[:, :], pr == 0, pr == 1,
                     after=[*free, *pt], inc=(n == 7 and pr == 1))
    IM, M8 = M.sb([128, 8, 16], ctx=s1), M.sb([128, 8, 8], ctx=s1)
    u = M.tt(IM[:, :, :], Q.t[:, bk[0], 0:128].rearrange("p (a b) -> p a b", a=8), FR[:, :, :], ADD, after=[t, *loads])
    Q.give(bk, [u])
    for n in range(8):
        u = M.V.put(lambda e, n=n: e.max(M8[:, n, :], IM[:, n, :]), [u])
        u = M.V.put(lambda e, n=n: e.match_replace(SELN[:, n, :], M8[:, n, :], IM[:, n, :], 3e38), [u])
    sel = M.ts(SELN[:, :, :], SELN[:, :, :], 1e38, ALU.is_lt, NEG, MUL, after=[u])
    s1.close()
    start = M.fence()
    s1 = Scope()
    GM = M.sb([128, 4, T], ctx=s1)
    WM = M.sb([128, 128], ctx=s1)
    ld2 = sem_of()
    for d, s in ((GM[:, :, :], A["c_causal"]), (WM[:, :], A["c_window"])):
        loads = [M.Y.load(lambda e, d=d, s=s: e.dma_start(d, s), ld2, 32, after=start)]
    SB = M.sb([128, 2, T], ctx=s1)
    WB = M.sb([128, 2, 384], ctx=s1)
    PS_ = M.sb([128, 2, T], ctx=s1)
    PW = M.sb([128, 2, 384], ctx=s1)
    st = M.sb([128, 2, 2, 4], ctx=s1)
    state = {"y": yw}
    keep = {}

    def attend(kind):
        buf, pbuf, K, v0 = ((SB, PS_, KS, 0), (WB, PW, KW, 64))[kind]
        it = 0
        for n in range(8):
            k0 = 0 if kind == 0 else max(0, n - 2)
            L = (n + 1 - k0) * 128
            off = 896 - 128 * (n - k0)
            for h in range(4):
                b = it % 2
                it += 1
                p = slice(64 * (h % 2), 64 * (h % 2) + 64)
                sv = st[:, kind, b, :]
                busy = keep.get((kind, b), [])
                for c0 in range(0, L, 512):
                    c1 = min(L, c0 + 512)
                    bk, free = Q.take(1)
                    t = M.mm(Q.t[:, bk[0], 0:c1 - c0], QF[p, h // 2, n * 128:n * 128 + 128], K[p, k0 * 128 + c0:k0 * 128 + c1], True, True,
                             after=[*free, *w[4], *w[5], *w[1], *w[2]], inc=True)
                    u = M.stt(buf[:, b, c0:c1], Q.t[:, bk[0], 0:c1 - c0], 0.125, GM[:, h, off + c0:off + c1], MUL, ADD, after=[t, *loads, *busy])
                    Q.give(bk, [u])
                if kind == 0:
                    g = buf[:, b, 0:L].rearrange("p (a b) -> p a b", b=64)
                    u = M.tt(g, g, SELN[:, n, 0:L // 64].unsqueeze(2).to_broadcast([128, L // 64, 64]), ADD, after=[u, sel])
                elif n >= 2:
                    u = M.tt(buf[:, b, 0:128], buf[:, b, 0:128], WM[:, :], ADD, after=[u, *loads])
                u = red(sv[:, 0:1], buf[:, b, 0:L], MAX, [u])
                u = M.ts(sv[:, 1:2], sv[:, 0:1], -1.0, MUL, after=[u])
                a = M.act(buf[:, b, 0:L], buf[:, b, 0:L], ACT.Exp, after=[u], bias=sv[:, 1:2], accum=sv[:, 2:3])
                yield
                u = M.recip(sv[:, 3:4], sv[:, 2:3], after=[a])
                rg = M.tt(sv[:, 3:4], sv[:, 3:4], small.gate[:, n, 3 * h + 1 + kind:3 * h + 2 + kind], MUL, after=[u])
                cps = []
                for c0 in range(0, L, 512):
                    c1 = min(L, c0 + 512)
                    bk, free = Q.take(1)
                    for i in range(c0, c1, 128):
                        t = M.tr(Q.t[:, bk[0], i - c0:i - c0 + 128], buf[:, b, i:i + 128], C.ident, after=[*free, a], inc=(i + 128 == c1))
                    cps.append(M.cp(pbuf[:, b, c0:c1], Q.t[:, bk[0], 0:c1 - c0], after=[t, *keep.get(("p", kind, b), [])]))
                    Q.give(bk, [cps[-1]])
                keep[(kind, b)] = [t]
                yield
                bk, free = Q.take(1)
                for i in range(L // 128):
                    t = M.mm(Q.t[:, bk[0], 0:64], pbuf[:, b, i * 128:i * 128 + 128], VSW[:, k0 + i, v0:v0 + 64], i == 0, i == L // 128 - 1,
                             after=[*free, *cps, vsw[0]], inc=(i == L // 128 - 1))
                y = Y[:, n, h * 64:h * 64 + 64]
                u = M.stt(y, Q.t[:, bk[0], 0:64], sv[:, 3:4], y, MUL, ADD, after=[t, rg, *state["y"]])
                Q.give(bk, [u])
                keep[("p", kind, b)] = [t]
                state["y"] = [u]
                yield
    yield from both(attend(0), attend(1))
    s1.close()
    M.fence()
    s1 = Scope()
    YF = M.sb([128, T], ctx=s1)
    ZZ = M.sb([128, T], ctx=s1)
    fill.align()
    for j in range(2):
        def evac2(m, ps, tok):
            w["z"] = [M.act(ZZ[:, :], ps, ACT.Silu, after=[tok, *state["y"]])]
            return w["z"]
        run(dense(M, W, P, hk, 1, evac2))
        for q in range(2):
            bk, free = Q.take(1)
            for i in range(4):
                t = M.tr(Q.t[:, bk[0], i * 128:i * 128 + 128], Y[:, 4 * q + i, j * 128:j * 128 + 128], C.ident, after=[*free, *state["y"]], inc=(i == 3))
            u = M.tt(YF[:, q * 512:q * 512 + 512], Q.t[:, bk[0], :], ZZ[:, q * 512:q * 512 + 512], MUL, after=[t, *w["z"]])
            Q.give(bk, [u])
        stored = [done(6 + j, YF[:, :], [u])]
        for e in (M.V, M.S, M.G):
            e.wait(stored)
    s1.close()
    s0.close()
    M.fence()


def hybrid(M, W, P, Q, C, A, X, vecs, at, keep_g, keep_y):
    vec = lambda n, i, k=1: vecs[:, at[n] + i:at[n] + i + k] if k == 1 else vecs[:, at[n]:at[n] + k]
    c2 = Scope("right")
    H = Split(M, 8, c2)
    norm_split(M, P, C, X.t, X.w, lambda i: vec("norm_gain", i), H)
    X.set_aside()
    hk = [(H.hi[:, i, :], H.lo[:, i, :], H.w[i]) for i in range(8)]
    c = Scope()
    names = ["c2", "rw_up", "sg_w", "sg_b"]
    lv = M.sb([128, 7 * 128 + 128 + 128 + 256], ctx=c, name="c2")
    C.rw_up = M.sb([128, 256], ctx=c, name="rwup")
    C.sg_w = M.sb([128, 4, 128], ctx=c, name="sgw")
    C.sg_b = M.sb([4, 128], ctx=c, name="sgb")
    s_k = M.newsem("s_k")
    start = M.fence()
    for d, s in zip((lv[:, :], C.rw_up[:, :], C.sg_w[:, :, :], C.sg_b[:, :]), names):
        ld = M.Y.load(lambda e, d=d, s=s: e.dma_start(d, A[s]), s_k, 64, after=[*start, *X.stored])
    small = Consts()
    small.rows = M.sb([76, T], ctx=c, name="rows")
    small.gT = M.sb([128, 8, 4], ctx=c, name="gt")
    small.gate = M.sb([128, 8, 12], ctx=c, name="gate")
    WA = M.sb([128, T], ctx=c, name="wa")
    ZY = M.sb([128, 2, T], ctx=c, name="zy")
    GS = M.sb([128, 2, T], ctx=c, name="gs")
    C.eps5, C.epsgn = M.sb([128, 1], ctx=c), M.sb([128, 1], ctx=c)
    t1, t2 = M.fill(C.eps5[:, :], 1e-5), M.fill(C.epsgn[:, :], 64e-5)
    for e in (M.T, M.V, M.S, M.G):
        e.wait([ld, t1, t2])
    t = M.tt(C.sg_w[:, :, :], C.sg_w[:, :, :], C.upper.unsqueeze(1).to_broadcast([128, 4, 128]), MUL)
    M.T.wait([t])
    C.level = [lv[:, b * 128:b * 128 + 128] for b in range(7)]
    C.heads = lv[:, 896:1024]
    C.strict = lv[:, 1024:1152]
    C.pair = lv[:, 1152:1408].rearrange("p (a b) -> p a b", a=2)
    gsem = [M.newsem("s_g0"), M.newsem("s_g1")]
    gout = {}

    def merge():
        def evac(m, ps, tok):
            b = m % 2
            t = M.act(GS[:, b, :], ps, ACT.Sigmoid, after=[tok, *gout.get(m - 2, [])])
            gout[m] = [M.Y.load(lambda e: e.dma_start(keep_g[m], GS[:, b, :]), gsem[b], 16 * (m // 2 + 1), after=[t])]
            return [t]
        yield from dense(M, W, P, hk, 32, evac, "merge")
    ysem = [M.newsem("s_y0"), M.newsem("s_y1")]
    yout = {}

    def done(i, src, after):
        b = i % 2
        yout[i] = M.Y.load(lambda e: e.dma_start(keep_y[i], src), ysem[b], 16 * (i // 2 + 1), after=after)
        return yout[i]

    with Scope() as ct:
        pad = M.sb([128, 1 + T], ctx=ct)
        tmp = M.sb([128, T], ctx=ct)
        r1, r2, r3, r4, r5 = (M.sb([4, T], ctx=ct) for _ in range(5))
        ea, dt = M.sb([4, 1], ctx=ct), M.sb([4, 1], ctx=ct)
        got = {}

        def evac(m, ps, tok):
            if m == 0:
                a = M.act(r1[:, :], ps[0:4], ACT.Identity, after=[tok], bias=vecs[0:4, at["gdn_small"] + 1:at["gdn_small"] + 2])
                b = M.act(small.rows[32:36, :], ps[32:36], ACT.Sigmoid)
                g = M.act(small.rows[64:76, :], ps[64:76], ACT.Sigmoid)
                got["t"] = [g]
                return [g]
            a = M.act(pad[:, 1:], ps, ACT.Copy, after=[tok])
            got["p"] = [a]
            return [a]
        run(dense(M, W, P, hk, 2, evac))
        e = M.act(ea[:, :], vecs[0:4, at["gdn_small"]:at["gdn_small"] + 1], ACT.Exp)
        u = M.ts(r1[:, :], r1[:, :], -1.0, MUL, after=got["t"])
        u = softplus_neg(M, r1[:, :], [x[:, :] for x in (r2, r3, r4, r5)], [u])
        u = M.ts(r1[:, :], r1[:, :], ea[:, 0:1], MUL, -1.0, MUL, after=[u, e])
        z = M.fill(r2[:, :], 0.0)
        for n in range(8):
            sl = slice(n * 128, n * 128 + 128)
            u = M.scan(small.rows[0:4, sl], r1[:, sl], r2[:, sl], 0.0, ADD, ADD, after=[u, z])
        for p, w, dst, after in ((slice(0, 4), 4, small.gT, [u]), (slice(64, 76), 12, small.gate, got["t"])):
            bk, free = Q.take(1)
            for n in range(8):
                t = M.tr(Q.t[:, bk[0], n * w:n * w + w], small.rows[p, n * 128:n * 128 + 128], C.ident[p, p], after=[*after, *free], inc=(n == 7))
            y = M.cp(dst[:, :, :], Q.t[:, bk[0], 0:8 * w].rearrange("p (a b) -> p a b", a=8), after=[t])
            Q.give(bk, [y])
        small.w = [u, y, *got["t"]]
        z = M.fill(pad[:, 0:1], 0.0)
        u = M.tt(tmp[:, :], pad[:, 0:T], pad[:, 1:], SUB, after=[z, *got["p"]])
        u = M.stt(WA[:, :], tmp[:, :], vec("rw_mu", 6), pad[:, 1:], MUL, ADD, after=[u])
        a = M.act(WA[0:64, :], WA[0:64, :], ACT.Tanh, after=[u])
        waw = [u, a]
        M.fence()
    fill = Filler(merge())
    rates = {0: 0.7, 1: 0.7, 2: 0.4, 3: 0.4, 4: 0.7, 5: 0.7}
    for i in range(6):
        j = i % 2
        zy = ZY[:, j, :]
        if i >= 2:
            M.S.wait([yout[i - 2]])
        if i < 2:
            g = gdn(M, W, P, Q, C, hk, j, zy, small, vec)
        elif i < 4:
            g = spatial(M, W, P, Q, C, hk, j, zy, small, vec)
        else:
            g = rwkv(M, W, P, Q, C, hk, j, zy, small, vec, WA, waw)
        fill.blend(g, rates[i])
        done(i, zy, small.y)
    sems = iter([M.newsem("s_n0"), M.newsem("s_n1")])
    fill.blend(nsa(M, W, P, Q, C, A, hk, small, vec, done, lambda: next(sems), fill), 0.3)
    run(fill.gen)
    for e in (M.V, M.S, M.G):
        e.wait([*yout.values(), *[t for v in gout.values() for t in v]])
    c.close()
    c2.close()
    start = M.fence()
    c3 = Scope()
    MX = M.sb([128, 8, T], ctx=c3, name="mx")
    with Scope("right") as c2:
        YS = Split(M, 8, c2)
        with Scope() as c4:
            YB = M.sb([128, 2, T], ctx=c4)
            GB = M.sb([128, 3, T], ctx=c4)
            TM = M.sb([128, 2, T], ctx=c4)
            ls = [M.newsem("s_l0"), M.newsem("s_l1")]
            gs = [M.newsem(f"s_m{i}") for i in range(3)]
            back = [*yout.values(), *[t for v in gout.values() for t in v], *start]
            rd = [[], []]
            for i in range(8):
                b = i % 2
                t = M.Y.load(lambda e, i=i, b=b: e.dma_start(YB[:, b, :], keep_y[i]), ls[b], 16 * (i // 2 + 1), after=[*back, *rd[b]])
                rd[b] = YS.store(M, i, YB[:, b, :], [t], eng=M.V if i % 2 else M.G)
            gl, gr = {}, {}

            def fetch(n):
                if n < 32:
                    s, i = n % 3, (n % 4) * 8 + n // 4
                    gl[n] = M.Y.load(lambda e: e.dma_start(GB[:, s, :], keep_g[i]), gs[s], 16 * (n // 3 + 1), after=[*back, *gr.get(n - 3, [])])
            for n in range(3):
                fetch(n)
            mw = {}
            tr_ = [[], []]
            for m in range(8):
                for i in range(4):
                    n = 4 * m + i

                    def evac(_, ps, tok):
                        if i == 0:
                            u = M.tt(MX[:, m, :], ps, GB[:, n % 3, :], MUL, after=[tok, gl[n]])
                            mw[m] = [u]
                        else:
                            u = M.tt(TM[:, n % 2, :], ps, GB[:, n % 3, :], MUL, after=[tok, gl[n], *tr_[n % 2]])
                            tr_[n % 2] = mw[m] = [M.tt(MX[:, m, :], MX[:, m, :], TM[:, n % 2, :], ADD, after=[u, *mw[m]], eng=M.G)]
                        gr[n] = [u]
                        fetch(n + 3)
                        return [u]
                    run(dense(M, W, P, [(YS.hi[:, k, :], YS.lo[:, k, :], YS.w[k]) for k in (2 * i, 2 * i + 1)], 1, evac))
            M.fence()
    with Scope("right") as c2:
        MS = Split(M, 8, c2)
        for i in range(8):
            MS.store(M, i, MX[:, i, :], mw[i], eng=M.V if i % 2 else M.G)
        c3.close()
        X.load()

        def evac(m, ps, tok):
            t = M.tt(X.t[:, m, :], X.t[:, m, :], ps, ADD, after=[tok, *X.w[m]])
            X.w[m] = [t]
            return [t]
        run(dense(M, W, P, [(MS.hi[:, i, :], MS.lo[:, i, :], MS.w[i]) for i in range(8)], 8, evac))
        M.fence()
    with Scope() as c:
        sq, rs = M.sb([128, 2, T], ctx=c), M.sb([128, T], ctx=c)
        r = rstd_rows(M, P, C, lambda i: X.t[:, i, :], 8, D, X.w, rs[:, :], sq)
        for i in range(8):
            X.w[i] = [M.stt(X.t[:, i, :], X.t[:, i, :], vec("final_gain", i), rs[:, :], MUL, MUL, after=[r])]
        M.fence()


OFF = dict(qkv=0, a=768, b=772, gz=776, su=1032, sv=1288, sz=1544, rw=1800, rz=2696, nq=2952, kv=3208, ng=3592, nz=3604, merge=3860)


def vector_layout2(inp, add):
    for n in ("norm_gain", "sg_ln_gain", "sg_ln_bias", "rw_mu", "rw_w0", "rw_a0", "rw_k_k", "rw_k_a", "rw_r_k", "rw_gn_gain", "rw_gn_bias"):
        add(n, inp[n + "_2"][0].reshape(-1, 128).T)
    add("final_gain", inp["final_gain_2"].reshape(-1, 128).T)
    g = inp["gdn_norm_2"][0]
    add("gdn_norm", np.concatenate([g, g]).reshape(128, 1))
    for m in range(6):
        add(f"gdn_conv{m}", inp["gdn_conv_2"][0][:, m * 128:(m + 1) * 128].T)
    a = np.zeros((128, 2), g.dtype)
    a[0:4, 0] = inp["gdn_a_log_2"][0]
    a[0:4, 1] = inp["gdn_dt_bias_2"][0]
    add("gdn_small", a)


def hybrid_blocks(inp, out):
    w = inp["w_in_2"][0]

    def cols(*parts, to=out):
        t = np.concatenate(parts, 1)
        to += [t[k * 128:(k + 1) * 128] for k in range(8)]

    def at(*offsets, to=out):
        for o in offsets:
            cols(w[:, o:o + 128], to=to)
    small = np.zeros((D, 128), w.dtype)
    small[:, 0:4] = w[:, OFF["a"]:OFF["a"] + 4]
    small[:, 32:36] = w[:, OFF["b"]:OFF["b"] + 4]
    small[:, 64:76] = w[:, OFF["ng"]:OFF["ng"] + 12]
    cols(small)
    at(OFF["rw"] + 768)
    for o in (0, 128):
        at(o, 256 + o, 512 + o, OFF["gz"] + o)
    for o in (0, 128):
        at(OFF["su"] + o, OFF["sv"] + o, OFF["sz"] + o)
    for o in (0, 128):
        at(OFF["rw"] + 256 + o, OFF["rw"] + o, OFF["rw"] + 512 + o, OFF["rz"] + o)
    kv = [w[:, OFF["kv"] + 64 * i:OFF["kv"] + 64 * i + 64] for i in range(6)]
    for a, b in ((0, 1), (2, 2), (4, 4), (3, 5)):
        cols(kv[a], kv[b])
    at(OFF["nq"], OFF["nq"] + 128, OFF["nz"], OFF["nz"] + 128)
    for m in range(8):
        for i in range(4):
            b = inp["w_branch_2"][0, i]
            out += [b[k * 128:(k + 1) * 128, m * 128:(m + 1) * 128] for k in range(2)]
    for m in range(8):
        out += [inp["w_out_2"][0][k * 128:(k + 1) * 128, m * 128:(m + 1) * 128] for k in range(8)]
    merge = []
    at(*[OFF["merge"] + 128 * m for m in range(32)], to=merge)
    return merge


def constants2():
    f = np.float32
    p, q = np.arange(128)[:, None], np.arange(128)[None, :]
    c2 = np.zeros((128, 1408), f)
    for b in range(7):
        w = 1 << b
        c2[:, b * 128:b * 128 + 128] = (p // (2 * w) == q // (2 * w)) & (q % (2 * w) >= w) & (p % (2 * w) < w)
    c2[:, 896:1024] = p // 64 == q // 64
    c2[:, 1024:1152] = p < q
    for j in range(2):
        for s in range(2):
            for r in (0, 32):
                c2[r + 2 * j + s, 1152 + j * 128 + 64 * s:1152 + j * 128 + 64 * s + 64] = 1.0
    slopes = np.array(SLOPES, f)
    t = (np.arange(8)[None, :] * 128 + np.arange(128)[:, None]).astype(f)
    end = (np.arange(64) * 16 + 31).astype(f)
    dist = t[:, :, None] - end
    seen = (dist >= 0) & (np.arange(64) < 63)
    bias = np.where(seen[:, :, None, :], -slopes[None, None, :, None] * dist[:, :, None, :], f(NEG)).astype(f)
    blk, cur = np.arange(16), t[:, :, None] // 64
    force = np.where(blk <= cur, np.where((blk == 0) | (blk == cur) | (blk == cur - 1), f(1e4), f(0)), f(NEG)).astype(f)
    cs, bs = np.arange(63) * 16, np.arange(16) * 64
    inter = np.clip(np.minimum(cs[:, None] + 32, bs[None, :] + 64) - np.maximum(cs[:, None], bs[None, :]), 0, None).astype(f) / 32
    inter = np.concatenate([inter, np.zeros((1, 16), f)])
    u = np.arange(T)[None, :] - 896
    d = (p - u).astype(f)
    causal = np.where(d[:, None, :] >= 0, -slopes[None, :, None] * d[:, None, :], f(NEG)).astype(f)
    window = np.where(p - (q - 256) < 256, f(0), f(NEG)).astype(f)
    return {"c2": c2, "c_bias": bias, "c_mask": seen.astype(f), "c_force": force, "c_inter": np.concatenate([inter, inter]),
            "c_causal": causal, "c_window": window}


def layout2(inp):
    w1, w2, pos = (inp[n][0] for n in ("nsa_cmp_w1_2", "nsa_cmp_w2_2", "nsa_cmp_pos_2"))
    w1 = np.concatenate([w1[i].reshape(32, 64, 64).transpose(1, 0, 2) for i in range(2)])
    pos = np.concatenate([pos[0].T, pos[1].T])
    w2 = np.concatenate([np.concatenate([w2[0], w2[0]], 1), np.concatenate([w2[1], w2[1]], 1)])
    return {"rw_up": np.concatenate([inp["rw_w_up_2"][0], inp["rw_a_up_2"][0]]), "sg_w": inp["sg_w_s_2"][0].transpose(2, 0, 1),
            "sg_b": inp["sg_b_s_2"][0], "cmp_w1": w1, "cmp_pos": pos, "cmp_w2": w2, **constants2()}


def vector_layout(inp):
    cols, at = [], {}

    def add(name, a):
        at[name] = sum(x.shape[1] for x in cols)
        cols.append(a)

    for n in VECTORS:
        a = inp[n[:-1]][int(n[-1])] if n[-1] in "01" and n not in inp else inp[n]
        a = a.reshape(-1, 128).T
        add(n, a)
    b = inp["ml_b_in"][0]
    add("ml_b_in", b[:3072].reshape(-1, 128).T)
    last = np.zeros((128, 1), b.dtype)
    last[0:8, 0] = b[3072:3080]
    last[32:40, 0] = b[3080:3088]
    add("ml_gate_b", last)
    for n in ("conf_conv_w", "lru_conv_w"):
        for j in range(4):
            add(f"{n}{j}", inp[n][0][:, j * 128:(j + 1) * 128].T)
    vector_layout2(inp, add)
    return np.ascontiguousarray(np.concatenate(cols, 1)), at


def weight_stream(inp):
    out = []

    def tile(w, m, ks=None):
        for k in ks if ks is not None else range(w.shape[0] // 128):
            b = w[k * 128:(k + 1) * 128, m * 128:(m + 1) * 128]
            out.append(b)

    def ffn_blocks(l):
        g, u, d = inp["ffn_w_gate"][l], inp["ffn_w_up"][l], inp["ffn_w_down"][l]
        n, first = 0, 0
        for _ in range(FG[0]):
            tile(g, n)
            tile(u, n)
            n += 1
        for i, size in enumerate(FG):
            more = FG[i + 1] if i + 1 < len(FG) else 0
            if more:
                tile(g, n)
                tile(u, n)
                n += 1
            for m in range(8):
                tile(d, m, range(first, first + size))
            first += size
            for _ in range(more - 1):
                tile(g, n)
                tile(u, n)
                n += 1

    w = inp["ab_w_in"][0]
    for j in range(4):
        tile(w, j)
        tile(w, 4 + j)
    for m in (12, 13, 14, 15, 8, 9, 10, 11):
        tile(w, m)
    for m in range(8):
        tile(inp["ab_w_out"][0], m)
    ffn_blocks(0)
    w = inp["ml_w_in"][0]
    gates = np.zeros((D, 128), w.dtype)
    gates[:, 0:8] = w[:, 3072:3080]
    gates[:, 32:40] = w[:, 3080:3088]
    tile(gates, 0)
    for j in range(4):
        for m in (j, 4 + j, 8 + 2 * j, 9 + 2 * j):
            tile(w, m)
    for m in range(8):
        tile(w, 16 + m)
    for m in range(8):
        tile(inp["ml_w_out"][0], m)
    ffn_blocks(1)
    merge = hybrid_blocks(inp, out)
    return {"main": out, "merge": merge}


def pack(order, lists):
    lists = {k: iter(v) for k, v in lists.items()}
    blocks = [next(lists[s]) for s in order]
    assert all(next(v, None) is None for v in lists.values())
    while len(blocks) % 8:
        blocks.append(np.zeros((128, 128), blocks[0].dtype))
    return np.stack([np.concatenate(blocks[i:i + 8], 1) for i in range(0, len(blocks), 8)])


def constants():
    k = np.zeros((128, 128 * 3 + 1024), np.float32)
    k[:, 0:128] = np.eye(128)
    k[:, 128:256] = 1.0
    k[:, 256:384] = np.triu(np.ones((128, 128)))
    for p in range(8):
        for r in (0, 32):
            k[p + r, 384 + p * 128:384 + (p + 1) * 128] = 1.0
    return k


def lru_weights(inp):
    a = np.zeros((128, 2, 4, 128), np.float32)
    for wi, n in enumerate(("lru_w_a", "lru_w_x")):
        for h in range(8):
            p = 64 * (h % 2)
            a[p:p + 64, wi, h // 2, p:p + 64] = inp[n][0, h]
    return a


def layout(inp):
    vec, at = vector_layout(inp)
    x = inp["x"][0].T.reshape(8, 128, T).transpose(1, 0, 2)
    out = {"x": x, "vec": vec, "const": constants(), "lru": lru_weights(inp), **layout2(inp)}
    return {k: np.ascontiguousarray(v) for k, v in out.items()}, at


def program(nc, A, at, stages=range(5)):
    with Scope() as ctx:
        M = Machine(nc, ctx)
        C = Consts()
        ps = ctx.enter_context(nc.psum_tensor("ps", [128, 8, 512], F32))
        P = Banks(ps, [(0, 1), (2, 3)])
        Q = Banks(ps, [(4,), (5,), (6,), (7,)])
        keep = nc.dram_tensor("x_keep", [128, 8, T], F32, kind="Internal").ap()
        keep_g = [nc.dram_tensor(f"g_keep{i}", [128, T], F32, kind="Internal").ap() for i in range(32)]
        keep_y = [nc.dram_tensor(f"y_keep{i}", [128, T], F32, kind="Internal").ap() for i in range(8)]
        nv = A["vec"].shape[1]
        vec = M.sb([128, nv], name="vec")
        const = M.sb([128, 128 * 3 + 1024], name="const")
        C.eps = M.sb([128, 1], name="eps")
        s_c = M.newsem("s_c")
        toks = []
        for n, (dst, src) in enumerate(((vec[:, :], A["vec"]), (const[:, :], A["const"]))):
            toks.append(M.Y.load(lambda e, dst=dst, src=src: e.dma_start(dst, src), s_c, 32))
        C.ready = [toks[-1]]
        t = M.fill(C.eps[:, :], EPS)
        for e in (M.T, M.V, M.S, M.G):
            e.wait([*C.ready, t])
        C.ident, C.ones, C.upper = const[:, 0:128], const[:, 128:256], const[:, 256:384]
        C.sel = const[:, 384:384 + 1024].rearrange("p (h m) -> p h m", h=8)
        C.ml_bi = vec[0:8, at["ml_gate_b"]:at["ml_gate_b"] + 1]
        C.ml_bf = vec[32:40, at["ml_gate_b"]:at["ml_gate_b"] + 1]
        taps = {"conf_conv_w": 31, "lru_conv_w": 4}
        C.cols = lambda n, j: vec[:, at[f"{n}{j}"]:at[f"{n}{j}"] + taps[n]]
        C.span = lambda n: vec[:, at[n]:at[n] + 4]
        pv = lambda n, i: vec[:, at[n] + i:at[n] + i + 1]
        X = Residual(M, A["x"], keep)
        W = Weights(M, A["w"])
        X.load()
        for s in stages:
            if s == 0:
                mixer0(M, W, P, C, A, X, pv)
            if s == 1:
                ffn(M, W, P, C, X, lambda i: pv("pre_ffn_g0", i), lambda i: pv("post_ffn_g0", i))
            if s == 2:
                mixer1(M, W, P, Q, C, X, pv)
            if s == 3:
                ffn(M, W, P, C, X, lambda i: pv("pre_ffn_g1", i), lambda i: pv("post_ffn_g1", i))
            if s == 4:
                hybrid(M, W, P, Q, C, A, X, vec, at, keep_g, keep_y)
        s_out = M.newsem("s_out")
        t = M.Y.load(lambda e: e.dma_start(A["out"], X.t[:, :, :]), s_out, 16, after=[x for w in X.w for x in w])
        M.Y.wait([t])
        X.ctx.close()
        block = ctx.enter_context(nc.Block())
        block.sync(M.Y.emit)
        block.tensor(M.T.emit)
        block.vector(M.V.emit)
        block.scalar(M.S.emit)
        block.gpsimd(M.G.emit)
    return W.order


def kernel(**inputs):
    import concourse.bacc as bacc
    from concourse.bass_utils import run_bass_kernel_spmd

    inp = {k: np.asarray(v) for k, v in inputs.items()}
    arrays, at = layout(inp)
    lists = weight_stream(inp)
    chunks = -(-sum(len(v) for v in lists.values()) // 8)
    nc = bacc.Bacc("TRN2", target_bir_lowering=False, num_devices=1)
    dt = mybir.dt.from_np(np.dtype(np.float32))
    A = {k: nc.dram_tensor(f"in_{k}_dram", v.shape, dt, kind="ExternalInput").ap() for k, v in arrays.items()}
    A["w"] = nc.dram_tensor("in_w_dram", (chunks, 128, 1024), dt, kind="ExternalInput").ap()
    A["out"] = nc.dram_tensor("out_0_dram", (128, 8, T), dt, kind="ExternalOutput").ap()
    order = program(nc, A, at)
    arrays["w"] = pack(order, lists)
    r = run_bass_kernel_spmd(nc, [{f"in_{k}_dram": v for k, v in arrays.items()}], core_ids=[0])
    out = r.results[0]["out_0_dram"]
    return np.ascontiguousarray(out.transpose(1, 0, 2).reshape(D, T).T)[None]
```
